# Optimizing a Trainium2 kernel written in Bass

```python
import math
import jax, jax.numpy as jnp
from jax import lax
import numpy as np

D_MODEL = 1024
BATCH = 1
SEQ = 128
DEPTH = 2
DEC_BATCH = 1
DEC_SEQ = 128
PAST_LEN = 128

GRID_W = 64
N_MIXERS = 2
EPS = 1e-6
D_RNN = 1280
LRU_BLOCKS = 16
LRU_BLOCK = D_RNN // LRU_BLOCKS
CONV_W = 4
CONV_LEFT = 2
LRU_C = 8.0
N_HEADS = 8
HEAD_DIM = 64
V_DIM = 2 * HEAD_DIM
QK_W = N_HEADS * 2 * HEAD_DIM
ROPE_PAIRS = HEAD_DIM // 4
ROPE_THETA = 10000.0
Q_BLOCK = 128
N_EXPERTS = 64
N_GROUPS = 8
TOPK_GROUPS = 4
TOP_K = 8
D_EXPERT = 256
D_SHARED = 256
ROUTED_SCALE = 2.5

kernel_name = 'hybrid_rglru_diffattn_moe_diffusion_step'

def rms_norm(x, g):
    xf = x.astype(jnp.float32)
    y = xf * lax.rsqrt(jnp.mean(xf * xf, axis=-1, keepdims=True) + EPS)
    return (y * g.astype(jnp.float32)).astype(x.dtype)

def modulation(cond, w, b):
    m = jax.nn.silu(cond) @ w + b
    return m.reshape(cond.shape[0], 1, 6, D_MODEL)

def modulate_in(x, g, shift, scale):
    return rms_norm(x, g) * (1.0 + scale) + shift

def residual_out(x, y, g, gate):
    return x + gate * rms_norm(y, g)

def centred_conv(x, w, b):
    t = x.shape[1]
    xp = jnp.pad(x, ((0, 0), (CONV_LEFT, CONV_W - 1 - CONV_LEFT), (0, 0)))
    y = b
    for j in range(CONV_W):
        y = y + xp[:, j:j + t] * w[j]
    return y

def block_diag(x, w, b):
    bsz, t = x.shape[:2]
    y = jnp.einsum('bthi,hij->bthj', x.reshape(bsz, t, LRU_BLOCKS, LRU_BLOCK), w)
    return y.reshape(bsz, t, D_RNN) + b

def rglru_scan(x, gate_w, gate_b, lam, h0, reverse):
    r = jax.nn.sigmoid(block_diag(x, gate_w[0], gate_b[0]).astype(jnp.float32))
    i = jax.nn.sigmoid(block_diag(x, gate_w[1], gate_b[1]).astype(jnp.float32))
    log_a = -LRU_C * r * jax.nn.softplus(-lam.astype(jnp.float32))
    a = jnp.exp(log_a)
    u = jnp.sqrt(-jnp.expm1(2.0 * log_a)) * (i * x.astype(jnp.float32))

    def step(h, au):
        a_t, u_t = au
        h = a_t * h + u_t
        return h, h

    h_last, hs = lax.scan(step, h0.astype(jnp.float32),
                          (jnp.swapaxes(a, 0, 1), jnp.swapaxes(u, 0, 1)), reverse=reverse)
    return jnp.swapaxes(hs, 0, 1).astype(x.dtype), h_last.astype(x.dtype)

def lru_mixer(h, h0_fwd, h0_bwd, w_in, conv_w, conv_b, gate_w, gate_b, lam, w_out):
    xb = h @ w_in
    gate = jax.nn.gelu(xb[..., :D_RNN])
    xr = centred_conv(xb[..., D_RNN:], conv_w, conv_b)
    y_f, h_f = rglru_scan(xr, gate_w[0], gate_b[0], lam[0], h0_fwd, False)
    y_b, h_b = rglru_scan(xr, gate_w[1], gate_b[1], lam[1], h0_bwd, True)
    return ((y_f + y_b) * gate) @ w_out, h_f, h_b

def axial_rope_tables(n):
    rows = n // GRID_W
    row = jnp.repeat(jnp.arange(rows, dtype=jnp.float32), GRID_W)
    col = jnp.tile(jnp.arange(GRID_W, dtype=jnp.float32), rows)
    freqs = ROPE_THETA ** (-jnp.arange(ROPE_PAIRS, dtype=jnp.float32) / ROPE_PAIRS)
    ar = row[:, None] * freqs
    ac = col[:, None] * freqs
    cos = jnp.concatenate([jnp.cos(ar), jnp.cos(ar), jnp.cos(ac), jnp.cos(ac)], axis=-1)
    sin = jnp.concatenate([jnp.sin(ar), jnp.sin(ar), jnp.sin(ac), jnp.sin(ac)], axis=-1)
    return cos, sin

def apply_rope(x, cos, sin):
    xs = x.reshape(x.shape[:-1] + (4, ROPE_PAIRS))
    rot = jnp.stack([-xs[..., 1, :], xs[..., 0, :], -xs[..., 3, :], xs[..., 2, :]],
                    axis=-2).reshape(x.shape)
    c = cos[None, :, None, None, :].astype(x.dtype)
    s = sin[None, :, None, None, :].astype(x.dtype)
    return x * c + rot * s

def diff_qkv(h, w_qkv):
    bsz, t = h.shape[:2]
    qkv = h @ w_qkv
    q = qkv[..., :QK_W].reshape(bsz, t, N_HEADS, 2, HEAD_DIM)
    k = qkv[..., QK_W:2 * QK_W].reshape(bsz, t, N_HEADS, 2, HEAD_DIM)
    v = qkv[..., 2 * QK_W:].reshape(bsz, t, N_HEADS, V_DIM)
    return q, k, v

def diff_lambda(lp, lam_init):
    lp = lp.astype(jnp.float32)
    return jnp.exp(jnp.sum(lp[0] * lp[1])) - jnp.exp(jnp.sum(lp[2] * lp[3])) + lam_init

def diff_attend(q, k, v, lam):
    bsz, tq = q.shape[:2]
    nb = tq // Q_BLOCK
    qb = jnp.moveaxis(q.reshape(bsz, nb, Q_BLOCK, N_HEADS, 2, HEAD_DIM), 1, 0)
    scale = HEAD_DIM ** -0.5

    def one_block(qblk):
        s = jnp.einsum('bqhcd,bkhcd->bhcqk', qblk, k, preferred_element_type=jnp.float32) * scale
        p = jax.nn.softmax(s, axis=-1)
        w = p[:, :, 0] - lam * p[:, :, 1]
        return jnp.einsum('bhqk,bkhe->bqhe', w.astype(v.dtype), v)

    o = lax.map(one_block, qb)
    return jnp.moveaxis(o, 0, 1).reshape(bsz, tq, N_HEADS, V_DIM)

def diff_out(o, g, lam_init, w_o):
    bsz, t = o.shape[:2]
    o = rms_norm(o, g) * (1.0 - lam_init)
    return o.reshape(bsz, t, N_HEADS * V_DIM) @ w_o

def moe(x, router, router_bias, w_gate, w_up, w_down, ws_gate, ws_up, ws_down):
    scores = jax.nn.sigmoid(x.astype(jnp.float32) @ router.astype(jnp.float32))
    sel = scores + router_bias.astype(jnp.float32)
    grp = sel.reshape(sel.shape[:-1] + (N_GROUPS, N_EXPERTS // N_GROUPS))
    gscore = jnp.sum(lax.top_k(grp, 2)[0], axis=-1)
    _, gidx = lax.top_k(gscore, TOPK_GROUPS)
    gmask = jnp.any(gidx[..., :, None] == jnp.arange(N_GROUPS), axis=-2)
    emask = jnp.repeat(gmask, N_EXPERTS // N_GROUPS, axis=-1)
    _, eidx = lax.top_k(jnp.where(emask, sel, -jnp.inf), TOP_K)
    wsel = jnp.take_along_axis(scores, eidx, axis=-1)
    wsel = wsel / jnp.sum(wsel, axis=-1, keepdims=True) * ROUTED_SCALE
    combine = jnp.sum(jax.nn.one_hot(eidx, N_EXPERTS, dtype=jnp.float32) * wsel[..., None], axis=-2)
    h = jax.nn.silu(jnp.einsum('btd,edf->btef', x, w_gate)) * jnp.einsum('btd,edf->btef', x, w_up)
    routed = jnp.einsum('btef,efd->btd', h * combine[..., None].astype(x.dtype), w_down)
    shared = (jax.nn.silu(x @ ws_gate) * (x @ ws_up)) @ ws_down
    return routed + shared

def setup_inputs(seed: int = 0) -> dict:
    key = jax.random.key(seed)
    ks = jax.random.split(key, 32)
    n_lru = (DEPTH + N_MIXERS - 1) // N_MIXERS
    n_attn = DEPTH // N_MIXERS
    D = D_MODEL

    def nrm(k, shape, scale):
        return jax.random.normal(k, shape, jnp.float32) * scale

    u = jax.random.uniform(ks[15], (n_lru, 2, D_RNN), jnp.float32, 0.9, 0.999)
    return {
        'x_prompt': nrm(ks[0], (BATCH, SEQ, D), 1.0),
        'x_sample': nrm(ks[1], (DEC_BATCH, DEC_SEQ, D), 1.0),
        'c': nrm(ks[2], (DEC_BATCH, D), 1.0),
        'state_lru': nrm(ks[3], (DEC_BATCH, n_lru, 2, D_RNN), 0.5),
        'cache_k': nrm(ks[4], (DEC_BATCH, n_attn, PAST_LEN, N_HEADS, 2 * HEAD_DIM), 1.0),
        'cache_v': nrm(ks[5], (DEC_BATCH, n_attn, PAST_LEN, N_HEADS, V_DIM), 1.0),
        'c_ctx': nrm(ks[6], (D,), 1.0),
        'mod_w': nrm(ks[7], (DEPTH, D, 6 * D), 0.5 * D ** -0.5),
        'mod_b': nrm(ks[8], (DEPTH, 6 * D), 0.02),
        'norm_g': 1.0 + nrm(ks[9], (DEPTH, 4, D), 0.05),
        'lru_w_in': nrm(ks[10], (n_lru, D, 2 * D_RNN), D ** -0.5),
        'lru_conv_w': nrm(ks[11], (n_lru, CONV_W, D_RNN), CONV_W ** -0.5),
        'lru_conv_b': nrm(ks[12], (n_lru, D_RNN), 0.02),
        'lru_gate_w': nrm(ks[13], (n_lru, 2, 2, LRU_BLOCKS, LRU_BLOCK, LRU_BLOCK), LRU_BLOCK ** -0.5),
        'lru_gate_b': nrm(ks[14], (n_lru, 2, 2, D_RNN), 0.1),
        'lru_lambda': jnp.log(u) - jnp.log1p(-u),
        'lru_w_out': nrm(ks[16], (n_lru, D_RNN, D), D_RNN ** -0.5),
        'attn_w_qkv': nrm(ks[17], (n_attn, D, 3 * QK_W), D ** -0.5),
        'attn_lambda': nrm(ks[18], (n_attn, 4, HEAD_DIM), 0.1),
        'attn_subln': 1.0 + nrm(ks[19], (n_attn, V_DIM), 0.05),
        'attn_w_o': nrm(ks[20], (n_attn, N_HEADS * V_DIM, D), (N_HEADS * V_DIM) ** -0.5),
        'moe_router': nrm(ks[21], (DEPTH, D, N_EXPERTS), D ** -0.5),
        'moe_router_bias': nrm(ks[22], (DEPTH, N_EXPERTS), 0.01),
        'moe_w_gate': nrm(ks[23], (DEPTH, N_EXPERTS, D, D_EXPERT), D ** -0.5),
        'moe_w_up': nrm(ks[24], (DEPTH, N_EXPERTS, D, D_EXPERT), D ** -0.5),
        'moe_w_down': nrm(ks[25], (DEPTH, N_EXPERTS, D_EXPERT, D), D_EXPERT ** -0.5),
        'shared_w_gate': nrm(ks[26], (DEPTH, D, D_SHARED), D ** -0.5),
        'shared_w_up': nrm(ks[27], (DEPTH, D, D_SHARED), D ** -0.5),
        'shared_w_down': nrm(ks[28], (DEPTH, D_SHARED, D), D_SHARED ** -0.5),
    }

def reference(x_prompt, x_sample, c, state_lru, cache_k, cache_v, c_ctx, mod_w, mod_b, norm_g,
              lru_w_in, lru_conv_w, lru_conv_b, lru_gate_w, lru_gate_b, lru_lambda, lru_w_out,
              attn_w_qkv, attn_lambda, attn_subln, attn_w_o,
              moe_router, moe_router_bias, moe_w_gate, moe_w_up, moe_w_down,
              shared_w_gate, shared_w_up, shared_w_down):
    bp = x_prompt.shape[0]
    bs = x_sample.shape[0]
    n_lat = x_sample.shape[1]
    past = cache_k.shape[2]
    cos, sin = axial_rope_tables(n_lat)
    xp, xs = x_prompt, x_sample
    new_lru, new_k, new_v = [], [], []
    for i in range(DEPTH):
        j = i // N_MIXERS
        mc = modulation(c_ctx[None], mod_w[i], mod_b[i])
        ms = modulation(c, mod_w[i], mod_b[i])
        hp = modulate_in(xp, norm_g[i, 0], mc[:, :, 0], mc[:, :, 1])
        hs = modulate_in(xs, norm_g[i, 0], ms[:, :, 0], ms[:, :, 1])
        if i % N_MIXERS == 0:
            lru_p = (lru_w_in[j], lru_conv_w[j], lru_conv_b[j], lru_gate_w[j], lru_gate_b[j],
                     lru_lambda[j], lru_w_out[j])
            h0 = jnp.zeros((bp, D_RNN), xp.dtype)
            yp, hf, hb = lru_mixer(hp, h0, h0, *lru_p)
            new_lru.append(jnp.stack([hf, hb], axis=1))
            ys, _, _ = lru_mixer(hs, state_lru[:, j, 0], state_lru[:, j, 1], *lru_p)
        else:
            lam_init = 0.8 - 0.6 * math.exp(-0.3 * i)
            lam = diff_lambda(attn_lambda[j], lam_init)
            q, k, v = diff_qkv(hp, attn_w_qkv[j])
            yp = diff_out(diff_attend(q, k, v, lam), attn_subln[j], lam_init, attn_w_o[j])
            new_k.append(k.reshape(bp, k.shape[1], N_HEADS, 2 * HEAD_DIM))
            new_v.append(v)
            q, k, v = diff_qkv(hs, attn_w_qkv[j])
            q = apply_rope(q, cos, sin)
            k = apply_rope(k, cos, sin)
            kc = cache_k[:, j].reshape(bs, past, N_HEADS, 2, HEAD_DIM)
            k_all = jnp.concatenate([kc, k], axis=1)
            v_all = jnp.concatenate([cache_v[:, j], v], axis=1)
            ys = diff_out(diff_attend(q, k_all, v_all, lam), attn_subln[j], lam_init, attn_w_o[j])
        xp = residual_out(xp, yp, norm_g[i, 1], mc[:, :, 2])
        xs = residual_out(xs, ys, norm_g[i, 1], ms[:, :, 2])
        moe_p = (moe_router[i], moe_router_bias[i], moe_w_gate[i], moe_w_up[i], moe_w_down[i],
                 shared_w_gate[i], shared_w_up[i], shared_w_down[i])
        fp = moe(modulate_in(xp, norm_g[i, 2], mc[:, :, 3], mc[:, :, 4]), *moe_p)
        fs = moe(modulate_in(xs, norm_g[i, 2], ms[:, :, 3], ms[:, :, 4]), *moe_p)
        xp = residual_out(xp, fp, norm_g[i, 3], mc[:, :, 5])
        xs = residual_out(xs, fs, norm_g[i, 3], ms[:, :, 5])
    new_state_lru = jnp.stack(new_lru, axis=1)
    new_cache_k = jnp.stack(new_k, axis=1)
    new_cache_v = jnp.stack(new_v, axis=1)
    return (xp, xs, new_state_lru, new_cache_k, new_cache_v)


_drawn_inputs = setup_inputs


def setup_inputs(seed=0):
    import zlib

    import numpy as np

    out = dict(_drawn_inputs(seed))
    spreads = {}
    factors = {}
    for name, (base, spread) in spreads.items():
        noise = np.random.default_rng([zlib.crc32(name.encode()), seed]).standard_normal(out[name].shape)
        drawn = base * np.exp(spread * noise) if base else spread * noise
        out[name] = __import__('jax').numpy.asarray(drawn.astype(out[name].dtype))
    for name, factor in factors.items():
        out[name] = (out[name] * factor).astype(out[name].dtype)
    return out
```

```python
import math
from collections import namedtuple
from contextlib import ExitStack

import numpy as np

import concourse.bass as bass
from concourse import mybir

F32 = mybir.dt.float32
I32 = mybir.dt.int32
U32 = mybir.dt.uint32
ALU = mybir.AluOpType
ACT = mybir.ActivationFunctionType
AX = mybir.AxisListType.X

P = 128
NS = 2
T = NS * P
D = 1024
KD = D // P
R = 1280
KR = R // P
BLK = 80
HALF = 640
H = 8
HD = 64
E = 64
NG = 8
TOPG = 4
F = 256
SLOTS = 64
XITEMS = T * 8 // SLOTS
ITEMS = E + XITEMS
PAIRS = E // 2
EPS = 1e-6
ROUTED = 2.5
BIG = 3.0e38
LAM0 = 0.8 - 0.6 * math.exp(-0.3)
SCALE = HD ** -0.5
RING = 4
SLOT = 6144

N_MOD, N_WIN, N_GATE, N_WOUT = 0, 16, 20, 24
N_ROUTER = (26, 102)
N_SHARED = (27, 103)
N_EXPERT = (28, 104)
N_QKV, N_WO = 92, 98

G_START = [0, 0, 128, 256, 384]
G_END = [256, 384, 512, 640, 640]
G_OFF = [0, 256, 640, 1024, 1408]
G_HALF = 1664
G_INPUTS = [[k for k in range(5) if G_START[k] <= c * P < G_END[k]] for c in range(5)]

C_ID, C_TRI, C_ONE, C_IOTA, C_E, C_EPS, C_COS, C_SIN = 0, 128, 256, 384, 448, 449, 450, 514
C_N = 578


def constants():
    c = np.zeros((P, C_N), np.float32)
    c[:, C_ID:C_ID + P] = np.eye(P)
    c[:, C_TRI:C_TRI + P] = np.triu(np.ones((P, P)))
    c[:, C_ONE:C_ONE + P] = 1.0
    c[:, C_IOTA:C_IOTA + 64] = np.arange(64)
    c[:, C_E] = np.arange(P)
    c[:, C_EPS] = EPS
    pairs = HD // 4
    freqs = (10000.0 ** (-np.arange(pairs, dtype=np.float32) / pairs)).astype(np.float32)
    t = np.arange(P)
    ar = (t // 64).astype(np.float32)[:, None] * freqs
    ac = (t % 64).astype(np.float32)[:, None] * freqs
    c[:, C_COS:C_COS + HD] = np.concatenate([np.cos(ar), np.cos(ar), np.cos(ac), np.cos(ac)], 1)
    c[:, C_SIN:C_SIN + HD] = np.concatenate([-np.sin(ar), np.sin(ar), -np.sin(ac), np.sin(ac)], 1)
    return c


SEMAPHORES = """
consts_loaded rows_loaded x_loaded bias_loaded lambda_loaded cache_loaded
dve_first slot0_loaded slot1_loaded slot2_loaded slot3_loaded
down0_loaded down1_loaded down2_loaded down3_loaded
gate0_loaded gate1_loaded gate2_loaded gate3_loaded gate_zeroed
vecs_turned vecs_ready cond_ready mod_done mods_ready dve_step act_step
rms_in xn_ready xT_turned hT_dve hT_act diag_ready ggb_summed ggb_ready
win_done gelu_ready xr_ready xc_ready gate_summed gates_ready tanh_exp_done q_ready m_ready
ix_ready u_ready dir_done decay_exp decay_ready yT_ready wout_half mixer_done
state_ready state_turned state_copied state_stored rms_out x_new
logits_done scores_ready xm_turned xm_dve xm_act sh_summed sh_silu sh_h sh_done
mask_ready ranks_done counts_done pos_ready nb_ready hi_done m_cols_ready ppT_turned ppT_ready
xtable_done xtable_ready
lam_sums lam_exp lam_ready qkv_summed qkv_act qkv_dve roped qk_turned qkT_act qkT_dve
sc_done nm_ready p_ready w_ready wt_turned wt_ready pv_done o_copied o_squared o_rms o_normed oT_turned
oT_act oT_dve wo_done kv_stored outputs_stored y_done
""".split()
PAIR_SEMAPHORES = """
s_ready sw_ready gathered xg_act xg_dve gu_done silu_ready h_ready h_turned hT_ready down_done
o_act o_dve wT_turned wT_ready scattered
""".split()
SEMAPHORES += PAIR_SEMAPHORES + [f"x{L}_{n}" for L in (0, 1) for n in ["loaded"] + PAIR_SEMAPHORES]


class Steps:

    def __init__(self, eng, sem):
        self.eng, self.sem, self.n = eng, sem, 0

    def keep(self, ins):
        ins.then_inc(self.sem, 1)
        self.n += 1

    def settle(self):
        self.eng.wait_ge(self.sem, self.n)


def slot_value(n):
    expert = [e for n0 in N_EXPERT for e in range(n0, n0 + E)]
    return sum(0 if N_GATE <= m < N_WOUT else 32 if m in expert else 48 for m in range(n % RING, n + 1, RING))


def trunk(nc, a, outs):
    y_prompt, y_sample, new_state, new_k, new_v = outs
    ctx = ExitStack()
    with ctx:
        def sb(name, shape, dt=F32):
            return ctx.enter_context(nc.sbuf_tensor(name, shape, dt))

        sem = {name: ctx.enter_context(nc.semaphore(name)) for name in SEMAPHORES}
        s = namedtuple("Signals", SEMAPHORES)(**sem)
        extra = [namedtuple("Extra", ["loaded"] + PAIR_SEMAPHORES)(
            *[sem[f"x{L}_{n}"] for n in ["loaded"] + PAIR_SEMAPHORES]) for L in (0, 1)]

        ring = sb("ring", [P, RING, SLOT])
        con = sb("con", [P, C_N])
        x = sb("x", [P, NS, D])
        hT = sb("hT", [P, KD, T])
        ggb = sb("ggb", [P, NS, D])
        diag = sb("diag", [P, 16, P])
        junk = sb("junk", [P, D])
        rows = sb("rows", [P, 4, P])
        vecs = sb("vecs", [P, 4, P])
        condT = sb("condT", [P, NS, KD])
        modT = sb("modT", [P, 2, 48, NS])
        amod = sb("amod", [P, 4, KD, NS])
        gg = sb("gg", [P, 4, KD, NS])
        stat = sb("stat", [P, 4, NS])
        bias = sb("bias", [P, 2, E])
        lamrow = sb("lamrow", [P, 4, HD])
        lam = sb("lam", [P, 8])
        W = sb("W", [P, 15440])
        PS = ctx.enter_context(nc.psum_tensor("PS", [P, 8, 512], F32))

        ident, tri, ones = con[:, C_ID:C_ID + P], con[:, C_TRI:C_TRI + P], con[:, C_ONE:C_ONE + P]
        iota, ecol, epsc = con[:, C_IOTA:C_IOTA + 64], con[:, C_E:C_E + 1], con[:, C_EPS:C_EPS + 1]
        Y = PS[:, 0:4, :].rearrange("p (s h) n -> p s (h n)", s=NS)

        class Carve:

            def __init__(self):
                self.at = 0

            def __call__(self, *shape):
                n = math.prod(shape)
                v = W[:, self.at:self.at + n]
                self.at += n
                assert self.at <= 15440
                if len(shape) == 2:
                    v = v.rearrange("p (a b) -> p a b", a=shape[0])
                if len(shape) == 3:
                    v = v.rearrange("p (a b c) -> p a b c", a=shape[0], b=shape[1])
                return v

        c = Carve()
        gel, xc = c(KR, T), c(KR, T)
        xpad_flat = c(KR * NS * 132)
        xpad = xpad_flat.rearrange("p (c s t) -> p c s t", c=KR, s=NS)
        Q = xpad_flat[:, 0:KR * T].rearrange("p (c t) -> p c t", c=KR)
        RA, IU, HF = c(KR, T), c(KR, T), c(KR, T)
        sq = sb("sq", [P, 2, T])
        sp = sb("sp", [P, 6, 2 * KR])
        hl = sb("hl", [P, 2, KR])
        hlT = sb("hlT", [2 * KR, P])
        c = Carve()
        xm, xg, hE, hT2, osb = c(NS, D), c(KD, P), c(F), c(2, P), c(D)
        S = [c(NS, P), c(NS, P)]
        Sw, wT = c(NS, P), c(T)
        posI, comI = c(ITEMS, NS), c(ITEMS, NS)
        shg, shh = c(2, T), c(2, T)
        scores, sel, masked, rep, mask, comb, pp = (c(NS, E) for _ in range(7))
        gtop = c(NS, NG, 8)
        gsc, gm8, idxf, gmask = c(NS, NG), c(NS, 8), c(NS, 8), c(NS, NG)
        eq = c(NS, NG, TOPG)
        wsum = c(NS, 2)
        nb = c(1, 8)
        M, bM = c(32), c(32)
        ppT, combT = c(T), c(T)
        sg = c(F)
        idx = sb("idx", [P, NS, 8], U32)
        xtab = sb("xtab", [1, 64], I32)
        c = Carve()
        qkv = c(3, NS, D)
        kv_c = c(2, D)
        qT, kT = c(H, NS, P), c(H, 3, P)
        ot = qkv[:, 0]
        
        oT = hT
        rope = hT[:, :, :].rearrange("p (w k) n -> p w (k n)", w=2)
        pr, wmix, wmT = c(2, 2, T), c(2, T), c(2, T)
        sst = sb("sst", [P, 5, 16, 2])


        def as_rows(v):
            return v.rearrange("(k p) -> k p", p=P)

        ROW_SOURCES = [
            (0, 0, 64, a["norm_g"].rearrange("i j (k p) -> (i j k) p", p=P)),
            (0, 64, KD, as_rows(a["c_ctx"])), (0, 72, KD, as_rows(a["c"][0])),
            (1, 0, 96, a["mod_b"].rearrange("i (m p) -> (i m) p", p=P)),
            (2, 0, 4 * KR, a["lru_conv_w"][0].rearrange("j (k p) -> (j k) p", p=P)),
            (2, 40, KR, as_rows(a["lru_conv_b"][0])),
            (2, 50, 4 * KR, a["lru_gate_b"][0].rearrange("d g (k p) -> (d g k) p", p=P)),
            (2, 90, 2 * KR, a["lru_lambda"][0].rearrange("d (k p) -> (d k) p", p=P)),
            (3, 0, 2 * KR, a["state_lru"][0, 0].rearrange("d (k p) -> (d k) p", p=P)),
            (3, 20, 1, a["attn_subln"])]
        ROW_LOADS = len(ROW_SOURCES)
        ROW_TILES = [(80, 0), (96, 80), (110, 176), (21, 286)]
        GATE_DMAS = 12

        def conv_w(t, c):
            return vecs[:, 2, t * KR + c:t * KR + c + 1]

        def conv_b(c):
            return vecs[:, 2, 40 + c:41 + c]

        def gate_bias(dg, c):
            return vecs[:, 2, 50 + dg * KR + c:51 + dg * KR + c]

        neglam = vecs[:, 2, 90:110]

        def bmod(n):
            return modT[:, n // 2, 24 * (n % 2):24 * (n % 2) + 8]

        junk2 = diag[:, :, :].rearrange("p (s k) n -> p s (k n)", s=NS)
        TURNS = []
        for st, dst in ((0, 2), (None, 0), (1, 1)):
            for half in range(2):
                cols, hs = slice(half * 512, (half + 1) * 512), slice(half * 4, half * 4 + 4)
                if st is not None:
                    TURNS.append((qkv[:, 0, st, cols], qT[:, hs, st, :]))
                TURNS.append(((qkv[:, 1, st] if st is not None else kv_c[:, 0])[:, cols], kT[:, hs, dst, :]))

        def slot(n):
            return ring[:, n % RING]

        def loaded(eng, n):
            eng.wait_ge(sem[f"slot{n % RING}_loaded"], slot_value(n))

        def gvec(i, j):
            return vecs[:, 0, (i * 4 + j) * KD:(i * 4 + j + 1) * KD]

        def bc(ap, axis, n):
            v = ap.unsqueeze(axis)
            shape = list(v.shape)
            shape[axis] = n
            return v.to_broadcast(shape)

        def ring_view(n, k, width):
            return slot(n)[:, 0:k * width].rearrange("p (k n) -> p k n", k=k)


        block = ctx.enter_context(nc.Block())

        @block.sync
        def _(eng):
            def load_rows(n, src, k, width):
                v = ring_view(n, k, width)
                done = sem[f"slot{n % RING}_loaded"]
                if k == 2:
                    pieces = [(slice(0, 1), slice(0, width)), (slice(1, 2), slice(0, width // 2)),
                              (slice(1, 2), slice(width // 2, width))]
                else:
                    cut = {8: (0, 3, 6, 8), 5: (0, 2, 4, 5)}[k]
                    pieces = [(slice(p, q), slice(0, width)) for p, q in zip(cut, cut[1:])]
                for rows_, cols in pieces:
                    eng.dma_start(v[:, rows_, cols], src[:, rows_, cols]).then_inc(done, 16)

            def load_gate_up(place, gate, up, done):
                v = ring[:, place, 0:4096].rearrange("p (k m f) -> p k m f", k=KD, m=2)
                for i, w in enumerate((gate, up)):
                    eng.dma_start(v[:, :, i, :], w.rearrange("(k p) f -> p k f", p=P)).then_inc(done, 16)

            def load_down(place, down, done):
                eng.dma_start(ring[:, place, 4096:6144].rearrange("p (c n) -> p c n", c=2),
                              down.rearrange("(c p) n -> p c n", p=P)).then_inc(done, 16)

            def slot_sem(n):
                return sem[f"slot{n % RING}_loaded"]

            def moe_loads(L, free_router, free_shared, free_first):
                eng.wait_ge(*free_router)
                load_rows(N_ROUTER[L], a["moe_router"][L].rearrange("(k p) n -> p k n", p=P), KD, E)
                eng.wait_ge(*free_shared)
                n = N_SHARED[L]
                load_gate_up(n % RING, a["shared_w_gate"][L], a["shared_w_up"][L], slot_sem(n))
                load_down(n % RING, a["shared_w_down"][L], slot_sem(n))
                for e in range(RING):
                    eng.wait_ge(*free_first[e])
                    load_gate_up(e, a["moe_w_gate"][L, e], a["moe_w_up"][L, e], slot_sem(e))
                    load_down(e, a["moe_w_down"][L, e], sem[f"down{e}_loaded"])
                with eng.Fori(1, E // RING) as it:
                    for i in range(2):
                        eng.wait_ge(s.gu_done, it * 2 + (L * PAIRS + i - 1))
                        for q in (2 * i, 2 * i + 1):
                            load_gate_up(q, a["moe_w_gate"][L, it * RING + q], a["moe_w_up"][L, it * RING + q],
                                         slot_sem(q))
                        eng.wait_ge(s.down_done, it * 4 + 2 * (L * PAIRS + i - 1))
                        for q in (2 * i, 2 * i + 1):
                            load_down(q, a["moe_w_down"][L, it * RING + q], sem[f"down{q}_loaded"])

            def extra_loads(L):
                xs = extra[L]
                eng.wait_ge(s.down_done, 2 * ((L + 1) * PAIRS - 1))
                eng.wait_ge(s.xtable_ready, L + 1)
                count = eng.value_load(xtab[0:1, 32:33], min_val=0, max_val=XITEMS)
                with eng.Fori(0, XITEMS // 2) as i:
                    with eng.If(i * 2 < count):
                        eng.wait_ge(xs.s_ready, i + 1)
                        for q in range(2):
                            e = eng.value_load(xtab[0:1, bass.ds(i * 2 + q, 1)], min_val=0, max_val=E - 1)
                            load_gate_up(q, a["moe_w_gate"][L, e], a["moe_w_up"][L, e], xs.loaded)
                            load_down(q, a["moe_w_down"][L, e], xs.loaded)

            for n in range(16):
                if n >= RING:
                    eng.wait_ge(s.mod_done, n - RING + 1)
                load_rows(n, a["mod_w"][n // 8].rearrange("(k p) n -> p k n", p=P)
                          [:, :, (n % 8) * 768:(n % 8 + 1) * 768], KD, 768)
            for j in range(4):
                eng.wait_ge(s.mod_done, 12 + j + 1)
                load_rows(N_WIN + j, a["lru_w_in"][0].rearrange("(k p) n -> p k n", p=P)
                          [:, :, j * HALF:(j + 1) * HALF], KD, HALF)
            for j in range(2):
                eng.wait_ge(s.gate_summed, KR * (j + 1))
                load_rows(N_WOUT + j, a["lru_w_out"][0].rearrange("(k p) n -> p k n", p=P)
                          [:, 5 * j:5 * j + 5, :], 5, D)
            moe_loads(0, (s.gate_summed, 3 * KR), (s.gate_summed, 4 * KR),
                      [(s.wout_half, 1), (s.mixer_done, 1), (s.logits_done, 1), (s.sh_done, 1)])
            extra_loads(0)
            for j in (2, 3, 0, 1, 4, 5):
                if j < 2:
                    eng.wait_ge(s.y_done, 1)
                elif j < 4:
                    eng.wait_ge(s.down_done, 2 * PAIRS)
                else:
                    eng.wait_ge(s.qkv_summed, 2 * (j - 3))
                load_rows(N_QKV + j, a["attn_w_qkv"][0].rearrange("(k p) n -> p k n", p=P)
                          [:, :, j * 512:(j + 1) * 512], KD, 512)
            for j in range(4):
                eng.wait_ge(s.qkv_summed, 2 * (j + 3))
                load_rows(N_WO + j, a["attn_w_o"][0].rearrange("(k p) n -> p k n", p=P)
                          [:, 2 * j:2 * j + 2, :], 2, D)
            moe_loads(1, (s.wo_done, 1), (s.wo_done, 2),
                      [(s.wo_done, 3), (s.mixer_done, 2), (s.logits_done, 2), (s.sh_done, 2)])
            extra_loads(1)
            eng.wait_ge(s.x_new, 8)
            eng.dma_start(y_prompt[0], x[:, 0, :]).then_inc(s.outputs_stored, 16)
            eng.dma_start(y_sample[0], x[:, 1, :]).then_inc(s.outputs_stored, 16)
            eng.wait_ge(s.outputs_stored, 32)
            eng.wait_ge(s.kv_stored, 32)
            eng.wait_ge(s.state_stored, 16)

        @block.gpsimd
        def _(eng):
            for j in range(4):
                d, g = divmod(j, 2)
                eng.wait_ge(s.win_done, 5 * (j + 1))
                store = ring[:, j, 0:2 * G_HALF]
                eng.memset(store, 0.0).then_inc(s.gate_zeroed, 1)
                eng.wait_ge(s.gate_zeroed, j + 1)
                store = store.rearrange("p (h n) -> p h n", h=2)
                src = a["lru_gate_w"][0, d, g].rearrange("(h b) i j -> b i h j", h=2)
                for b in range(8):
                    r = b * BLK
                    while r < (b + 1) * BLK:
                        k = r // P
                        end = min((k + 1) * P, (b + 1) * BLK)
                        col = G_OFF[k] + b * BLK - G_START[k]
                        eng.dma_start(store[r - k * P:end - k * P, :, col:col + BLK],
                                      src[b, r - b * BLK:end - b * BLK]).then_inc(sem[f"gate{j}_loaded"], 16)
                        r = end
            for d in range(2):
                eng.wait_ge(s.gates_ready, 2 * KR * (d + 1))
                eng.wait_ge(s.xc_ready, KR)
                eng.tensor_tensor(IU, IU, xc, ALU.mult).then_inc(s.ix_ready, 1)
            eng.wait_ge(s.state_copied, 1)
            eng.dma_start(new_state[0, 0].rearrange("d (c p) -> (d c) p", p=P), hlT[:, :])\
               .then_inc(s.state_stored, 16)
            eng.wait_ge(s.qkv_act, 6)
            eng.dma_start(new_k[0, 0].rearrange("t h e -> t (h e)"), qkv[:, 1, 0]).then_inc(s.kv_stored, 16)
            eng.dma_start(new_v[0, 0].rearrange("t h e -> t (h e)"), qkv[:, 2, 0]).then_inc(s.kv_stored, 16)

        @block.tensor
        def _(eng):
            def mm(out, lhsT, rhs, first, last):
                return eng.matmul(out, lhsT, rhs, start=first, stop=last, skip_group_check=True)

            def norm_in(n):
                for b in range(4):
                    st, half = divmod(b, 2)
                    eng.wait_ge(s.xn_ready, 2 * n + st + 1)
                    for i in range(4):
                        k = half * 4 + i
                        ins = eng.transpose(PS[:, 4 + b, i * P:(i + 1) * P],
                                            junk2[:, st, k * P:(k + 1) * P], ident)
                    ins.then_inc(s.xT_turned, 1)
                eng.wait_ge(s.hT_dve, 2 * (n + 1))
                eng.wait_ge(s.hT_act, 2 * (n + 1))

            def sum_ggb(n):
                for b in range(4):
                    eng.wait_ge(s.diag_ready, 4 * n + b + 1)
                    for i in range(4):
                        ins = mm(PS[:, 4 + b, i * P:(i + 1) * P], ones, diag[:, 4 * b + i, :], i == 0, True)
                    ins.then_inc(s.ggb_summed, 1)
                eng.wait_ge(s.ggb_ready, 4 * (n + 1))

            eng.wait_ge(s.consts_loaded, 16)
            eng.wait_ge(s.rows_loaded, 16 * ROW_LOADS)
            for i, (n, at) in enumerate(ROW_TILES):
                ins = eng.transpose(PS[:, 7, at:at + n], rows[0:n, i, :], ident[0:n, 0:n])
            ins.then_inc(s.vecs_turned, 1)

            eng.wait_ge(s.cond_ready, 1)
            for n in range(16):
                L, blk = divmod(n, 8)
                loaded(eng, n)
                w = ring_view(n, KD, 768)
                for j in range(6):
                    m = blk * 6 + j
                    for k in range(KD):
                        ins = mm(PS[:, 5 + L, 2 * m:2 * m + 2], w[:, k, j * P:(j + 1) * P], condT[:, :, k],
                                 k == 0, k == KD - 1)
                ins.then_inc(s.mod_done, 1)

            norm_in(0)
            for c in range(2 * KR):
                n = N_WIN + c // 5
                loaded(eng, n)
                if 4 <= c < 14:
                    eng.wait_ge(s.gelu_ready, c - 3)
                elif c >= 14:
                    eng.wait_ge(s.xr_ready, c - 13)
                w = ring_view(n, KD, HALF)
                for k in range(KD):
                    ins = mm(PS[:, c % 4, 0:T], w[:, k, c % 5 * P:(c % 5 + 1) * P], hT[:, k, :],
                             k == 0, k == KD - 1)
                ins.then_inc(s.win_done, 1)
            sum_ggb(0)
            eng.wait_ge(s.xc_ready, KR)
            for j in range(4):
                eng.wait_ge(sem[f"gate{j}_loaded"], 16 * GATE_DMAS)
                store = ring[:, j, 0:2 * G_HALF].rearrange("p (h n) -> p h n", h=2)
                for c in range(KR):
                    i = j * KR + c
                    if i >= 4:
                        eng.wait_ge(s.gates_ready, i - 3)
                    half, cc = divmod(c, 5)
                    for k in G_INPUTS[cc]:
                        at = G_OFF[k] + cc * P - G_START[k]
                        ins = mm(PS[:, 4 + i % 4, 0:T], store[:, half, at:at + P], xc[:, half * 5 + k, :],
                                 k == G_INPUTS[cc][0], k == G_INPUTS[cc][-1])
                    ins.then_inc(s.gate_summed, 1)
            eng.wait_ge(s.state_ready, 1)
            eng.wait_ge(s.gates_ready, 4 * KR)
            eng.transpose(PS[0:2 * KR, 7, 0:P], hl[:, :, :].rearrange("p d c -> p (d c)"), ident)\
               .then_inc(s.state_turned, 1)
            for c in range(KR):
                loaded(eng, N_WOUT + c // 5)
                eng.wait_ge(s.yT_ready, c + 1)
                w = ring_view(N_WOUT + c // 5, 5, D)
                for st in range(NS):
                    for half in range(2):
                        ins = mm(PS[:, 2 * st + half, :], gel[:, c, st * P:(st + 1) * P],
                                 w[:, c % 5, half * 512:(half + 1) * 512], c == 0, c == KR - 1)
                if c == 4:
                    ins.then_inc(s.wout_half, 1)
                if c == KR - 1:
                    ins.then_inc(s.mixer_done, 1)

            def gather(sg_, j, Sb):
                eng.wait_ge(sg_.s_ready, j + 1)
                for half in range(2):
                    for i in range(4):
                        k = half * 4 + i
                        for st in range(NS):
                            ins = mm(PS[:, 6 + half, i * P:(i + 1) * P], xm[:, st, k * P:(k + 1) * P],
                                     Sb[:, st, :], st == 0, st == 1)
                    ins.then_inc(sg_.gathered, 1)

            def gate_up(sg_, j, places, wait_loaded):
                eng.wait_ge(sg_.xg_act, j + 1)
                eng.wait_ge(sg_.xg_dve, j + 1)
                wait_loaded(0)
                wait_loaded(1)
                for k in range(KD):
                    for e in range(2):
                        w = ring[:, places[e], k * 512:(k + 1) * 512]
                        ins = mm(PS[e * 64:(e + 1) * 64, 6, :], xg[:, k, e * 64:(e + 1) * 64], w,
                                 k == 0, k == KD - 1)
                ins.then_inc(sg_.gu_done, 1)

            def turn_hidden(sg_, j):
                eng.wait_ge(sg_.h_ready, j + 1)
                for fc in range(2):
                    ins = eng.transpose(PS[:, 7, fc * P:(fc + 1) * P], hE[:, fc * P:(fc + 1) * P], ident)
                ins.then_inc(sg_.h_turned, 1)

            def down(sg_, j, places, wait_loaded):
                eng.wait_ge(sg_.hT_ready, j + 1)
                wait_loaded(0)
                wait_loaded(1)
                for half in range(2):
                    for fc in range(2):
                        for e in range(2):
                            at = 4096 + fc * D + half * 512
                            ins = mm(PS[e * 64:(e + 1) * 64, 4 + half, :], hT2[:, fc, e * 64:(e + 1) * 64],
                                     ring[:, places[e], at:at + 512], fc == 0, fc == 1)
                    ins.then_inc(sg_.down_done, 1)

            def turn_weights(sg_, j, next_gathered):
                eng.wait_ge(sg_.sw_ready, j + 1)
                if next_gathered:
                    eng.wait_ge(sg_.xg_dve, j + 2)
                for st in range(NS):
                    ins = eng.transpose(PS[:, 7, 256 + st * P:256 + (st + 1) * P], Sw[:, st, :], ident)
                ins.then_inc(sg_.wT_turned, 1)

            def scatter(sg_, j, st):
                eng.wait_ge(sg_.o_act, j + 1)
                eng.wait_ge(sg_.o_dve, j + 1)
                eng.wait_ge(sg_.wT_ready, j + 1)
                for half in range(2):
                    ins = mm(PS[:, 2 * st + half, :], wT[:, st * P:(st + 1) * P],
                             osb[:, half * 512:(half + 1) * 512], False, False)
                ins.then_inc(sg_.scattered, 1)

            def moe(L):
                n = 2 * L + 1
                norm_in(n)
                loaded(eng, N_ROUTER[L])
                w = ring_view(N_ROUTER[L], KD, E)
                for st in range(NS):
                    for k in range(KD):
                        ins = mm(PS[:, 4, st * E:(st + 1) * E], hT[:, k, st * P:(st + 1) * P], w[:, k, :],
                                 k == 0, k == KD - 1)
                ins.then_inc(s.logits_done, 1)
                for b in range(4):
                    st, half = divmod(b, 2)
                    if b == 3:
                        eng.wait_ge(s.xm_dve, 2 * L + 1)
                    for i in range(4):
                        k = half * 4 + i
                        ins = eng.transpose(PS[:, (5, 6, 7, 5)[b], i * P:(i + 1) * P],
                                            hT[:, k, st * P:(st + 1) * P], ident)
                    ins.then_inc(s.xm_turned, 1)
                eng.wait_ge(s.scores_ready, L + 1)
                eng.wait_ge(s.xm_dve, 2 * (L + 1))
                eng.wait_ge(s.xm_act, 2 * (L + 1))
                sum_ggb(n)
                loaded(eng, N_SHARED[L])
                w = slot(N_SHARED[L])[:, 0:4096].rearrange("p (k m f) -> p m k f", m=2, k=KD)
                for fc in range(2):
                    for m in range(2):
                        for k in range(KD):
                            ins = mm(PS[:, 4 + 2 * fc + m, 0:T], w[:, m, k, fc * P:(fc + 1) * P], hT[:, k, :],
                                     k == 0, k == KD - 1)
                    ins.then_inc(s.sh_summed, 1)
                eng.wait_ge(s.sh_h, 2 * (L + 1))
                eng.wait_ge(s.mask_ready, L + 1)
                mm(PS[:, 4, 0:E], tri, mask[:, 0, :], True, True)
                mm(PS[:, 4, E:2 * E], ones, mask[:, 0, :], True, False)
                mm(PS[:, 4, E:2 * E], tri, mask[:, 1, :], False, True).then_inc(s.ranks_done, 1)
                mm(PS[0:E, 5, 0:1], mask[:, 0, :], ones[:, 0:1], True, False)
                mm(PS[0:E, 5, 0:1], mask[:, 1, :], ones[:, 0:1], False, True).then_inc(s.counts_done, 1)
                w = slot(N_SHARED[L])[:, 4096:6144].rearrange("p (c n) -> p c n", c=2)
                for st in range(NS):
                    for half in range(2):
                        for fc in range(2):
                            ins = mm(PS[:, 2 * st + half, :], shh[:, fc, st * P:(st + 1) * P],
                                     w[:, fc, half * 512:(half + 1) * 512], fc == 0, False)
                ins.then_inc(s.sh_done, 1)
                eng.wait_ge(s.nb_ready, L + 1)
                mm(PS[0:E, 6, 0:1], tri[0:E, 0:E], nb[0:E, 0, 4:5], True, True)
                mm(PS[0:1, 6, 8:9], nb[0:E, 0, 4:5], ones[0:E, 0:1], True, True).then_inc(s.hi_done, 1)
                eng.wait_ge(s.pos_ready, L + 1)
                for st in range(NS):
                    eng.transpose(PS[0:E, 7, st * P:(st + 1) * P], pp[:, st, :], ident)
                    ins = eng.transpose(PS[0:E, 7, 256 + st * P:256 + (st + 1) * P], comb[:, st, :], ident)
                ins.then_inc(s.ppT_turned, 1)
                eng.wait_ge(s.m_cols_ready, L + 1)
                eng.wait_ge(s.ppT_ready, L + 1)
                mm(PS[0:1, 6, 16:48], ecol[0:E, :], M[0:E, :], True, True)
                for st in range(NS):
                    mm(PS[:, 5, st * 32:(st + 1) * 32], ppT[0:E, st * P:(st + 1) * P], M[0:E, :], True, False)
                    mm(PS[:, 5, st * 32:(st + 1) * 32], ones[0:E, :], bM[0:E, :], False, True)
                    ins = mm(PS[:, 5, 64 + st * 32:64 + (st + 1) * 32], combT[0:E, st * P:(st + 1) * P],
                             M[0:E, :], True, True)
                ins.then_inc(s.xtable_done, 1)
                eng.wait_ge(s.xtable_ready, L + 1)

                def group(it, first, last):
                    for i in range(2):
                        j = L * PAIRS + it * 2 + i
                        places = (2 * i, 2 * i + 1)
                        more = not (last and i == 1)
                        gate_up(s, j, places, lambda e: eng.wait_ge(
                            sem[f"slot{places[e]}_loaded"], it * 32 + slot_value(N_EXPERT[L] + places[e])))
                        if not (first and i == 0):
                            scatter(s, j - 1, 0)
                        turn_hidden(s, j)
                        if not (first and i == 0):
                            scatter(s, j - 1, 1)
                        if more:
                            eng.wait_ge(s.hT_ready, j + 1)
                            gather(s, j + 1, S[(i + 1) % 2])
                        down(s, j, places, lambda e: eng.wait_ge(
                            sem[f"down{places[e]}_loaded"], it * 16 + (L * 256 + 16)))
                        turn_weights(s, j, more)

                gather(s, L * PAIRS, S[0])
                group(0, True, False)
                with eng.Fori(1, PAIRS // 2 - 1) as it:
                    group(it, False, False)
                group(PAIRS // 2 - 1, False, True)
                for st in range(NS):
                    scatter(s, (L + 1) * PAIRS - 1, st)
                xs = extra[L]
                count = eng.value_load(xtab[0:1, 32:33], min_val=0, max_val=XITEMS)
                with eng.Fori(0, XITEMS // 2) as i:
                    with eng.If(i * 2 < count):
                        gather(xs, i, S[0])
                        gate_up(xs, i, (0, 1), lambda e: eng.wait_ge(xs.loaded, i * 96 + 96))
                        turn_hidden(xs, i)
                        down(xs, i, (0, 1), lambda e: None)
                        turn_weights(xs, i, False)
                        for st in range(NS):
                            scatter(xs, i, st)
                mm(PS[:, 7, 0:64], ident, ones[:, 0:64], True, True).then_inc(s.y_done, 1)

            moe(0)

            norm_in(2)
            for j in range(6):
                loaded(eng, N_QKV + j)
                w = ring_view(N_QKV + j, KD, 512)
                for st in range(NS):
                    if j >= 2:
                        eng.wait_ge((s.qkv_act, s.qkv_dve)[st], j - 1)
                    for k in range(KD):
                        ins = mm(PS[:, (2 * j + st) % 4, :], hT[:, k, st * P:(st + 1) * P], w[:, k, :],
                                 k == 0, k == KD - 1)
                    ins.then_inc(s.qkv_summed, 1)
            sum_ggb(2)
            eng.wait_ge(s.qkv_act, 6)
            eng.wait_ge(s.qkv_dve, 6)
            eng.wait_ge(s.cache_loaded, 32)
            for g, (src, _) in enumerate(TURNS):
                if g >= 4:
                    eng.wait_ge((s.qkT_act, s.qkT_dve)[g % 2], g // 2 - 1)
                if g == 6:
                    eng.wait_ge(s.roped, 1)
                for i in range(4):
                    ins = eng.transpose(PS[:, 4 + g % 4, i * P:(i + 1) * P], src[:, i * P:(i + 1) * P], ident)
                ins.then_inc(s.qk_turned, 1)
            eng.wait_ge(s.qkT_act, 5)
            eng.wait_ge(s.qkT_dve, 5)
            for step in range(NS * H + 2):
                if step < NS * H:
                    j = step
                    st, h = divmod(j, H)
                    if j >= 2:
                        eng.wait_ge(s.p_ready, 2 * (j - 1))
                    for comp in range(2):
                        lo = comp * HD
                        keys = kT[lo:lo + HD, h, 2, :] if st == 0 else \
                            kT[lo:lo + HD, h, 0:2, :].rearrange("p a t -> p (a t)")
                        ins = mm(PS[:, 2 * (j % 2) + comp, 0:P * (st + 1)], qT[lo:lo + HD, h, st, :], keys,
                                 True, True)
                    ins.then_inc(s.sc_done, 1)
                if 1 <= step <= NS * H:
                    j = step - 1
                    eng.wait_ge(s.w_ready, j + 1)
                    for kt in range(j // H + 1):
                        ins = eng.transpose(PS[:, 4 + j % 2, kt * P:(kt + 1) * P],
                                            wmix[:, j % 2, kt * P:(kt + 1) * P], ident)
                    ins.then_inc(s.wt_turned, 1)
                if step >= 2:
                    j = step - 2
                    st, h = divmod(j, H)
                    eng.wait_ge(s.wt_ready, j + 1)
                    if j >= 2:
                        eng.wait_ge(s.o_copied, j - 1)
                    vals = [qkv[:, 2, 0]] if st == 0 else [kv_c[:, 1], qkv[:, 2, 1]]
                    for kt, v in enumerate(vals):
                        ins = mm(PS[:, 6 + j % 2, 0:P], wmT[:, j % 2, kt * P:(kt + 1) * P],
                                 v[:, h * P:(h + 1) * P], kt == 0, kt == len(vals) - 1)
                    ins.then_inc(s.pv_done, 1)
            for b in range(4):
                st, half = divmod(b, 2)
                eng.wait_ge(s.o_normed, 1)
                for i in range(4):
                    h = half * 4 + i
                    ins = eng.transpose(PS[:, 4 + b, i * P:(i + 1) * P], ot[:, st, h * P:(h + 1) * P], ident)
                ins.then_inc(s.oT_turned, 1)
            eng.wait_ge(s.oT_act, 2)
            eng.wait_ge(s.oT_dve, 2)
            for j in range(4):
                loaded(eng, N_WO + j)
                w = ring_view(N_WO + j, 2, D)
                for hh in range(2):
                    h = 2 * j + hh
                    for st in range(NS):
                        for half in range(2):
                            ins = mm(PS[:, 2 * st + half, :], oT[:, h, st * P:(st + 1) * P],
                                     w[:, hh, half * 512:(half + 1) * 512], h == 0, h == H - 1)
                ins.then_inc(s.wo_done if j < 3 else s.mixer_done, 1)
            moe(1)

        @block.scalar
        def _(eng):
            act = Steps(eng, s.act_step)

            eng.dma_start(con[:, :], a["constants"]).then_inc(s.consts_loaded, 16)
            for tile_, at, n, src in ROW_SOURCES:
                eng.dma_start(rows[at:at + n, tile_, :], src).then_inc(s.rows_loaded, 16)
            eng.dma_start(x[:, 0, :], a["x_prompt"][0]).then_inc(s.x_loaded, 16)
            eng.dma_start(x[:, 1, :], a["x_sample"][0]).then_inc(s.x_loaded, 16)
            eng.dma_start(bias[:, :, :], a["moe_router_bias"].partition_broadcast(P)).then_inc(s.bias_loaded, 16)
            eng.dma_start(lamrow[:, :, :], a["attn_lambda"][0].partition_broadcast(P))\
               .then_inc(s.lambda_loaded, 16)

            def norm_in(n):
                if n == 0:
                    eng.wait_ge(s.x_loaded, 32)
                    eng.wait_ge(s.consts_loaded, 16)
                else:
                    eng.wait_ge(s.x_new, 2 * n)
                for st in range(NS):
                    act.settle()
                    act.keep(eng.activation(junk[:, :], x[:, st, :], ACT.Square, accum_out=stat[:, 0, st:st + 1]))
                act.settle()
                eng.activation(stat[:, 1, :], stat[:, 0, :], ACT.Sqrt, scale=1.0 / D, bias=epsc).then_inc(s.rms_in, 1)
                if n == 0:
                    eng.wait_ge(s.mods_ready, 1)
                for b in (1, 3):
                    st, half = divmod(b, 2)
                    eng.wait_ge(s.xT_turned, 4 * n + b + 1)
                    for i in range(4):
                        k = half * 4 + i
                        ins = eng.activation(hT[:, k, st * P:(st + 1) * P], PS[:, 4 + b, i * P:(i + 1) * P],
                                             ACT.Identity, scale=amod[:, n, k, st:st + 1],
                                             bias=bmod(n)[:, k, st:st + 1])
                    ins.then_inc(s.hT_act, 1)

            def copy_ggb(n):
                for b in range(4):
                    eng.wait_ge(s.ggb_summed, 4 * n + b + 1)
                    eng.copy(ggb[:, b // 2, b % 2 * 512:(b % 2 + 1) * 512], PS[:, 4 + b, :]).then_inc(s.ggb_ready, 1)

            def norm_out(n):
                eng.wait_ge(s.mixer_done if n % 2 == 0 else s.y_done, n // 2 + 1)
                for st in range(NS):
                    act.settle()
                    act.keep(eng.activation(junk[:, :], Y[:, st, :], ACT.Square, accum_out=stat[:, 2, st:st + 1]))
                act.settle()
                eng.activation(stat[:, 3, :], stat[:, 2, :], ACT.Sqrt, scale=1.0 / D, bias=epsc)\
                   .then_inc(s.rms_out, 1)

            eng.wait_ge(s.vecs_ready, 1)
            eng.activation(condT[:, :, :].rearrange("p s k -> p (s k)"), vecs[:, 0, 64:80], ACT.Silu)\
               .then_inc(s.cond_ready, 1)
            eng.wait_ge(s.dve_first, 2)
            eng.activation(sp[:, 1, :], sp[:, 0, :], ACT.Exp).then_inc(s.decay_exp, 1)
            eng.activation(lam[:, 2:4], lam[:, 0:2], ACT.Exp).then_inc(s.lam_exp, 1)
            norm_in(0)
            for c in range(KR):
                eng.wait_ge(s.win_done, c + 1)
                eng.activation(gel[:, c, :], PS[:, c % 4, 0:T], ACT.Gelu_apprx_tanh).then_inc(s.gelu_ready, 1)
            copy_ggb(0)
            for d in range(2):
                if d:
                    eng.wait_ge(s.dir_done, 1)
                for g in range(2):
                    for c in range(KR):
                        i = (2 * d + g) * KR + c
                        eng.wait_ge(s.gate_summed, i + 1)
                        eng.activation((RA, IU)[g][:, c, :], PS[:, 4 + i % 4, 0:T], ACT.Sigmoid,
                                       bias=gate_bias(2 * d + g, c)).then_inc(s.gates_ready, 1)
                eng.wait_ge(s.decay_ready, 1)
                eng.wait_ge(s.xc_ready, KR)
                eng.wait_ge(s.gates_ready, (2 * d + 1) * KR)
                for c in range(KR):
                    la = sp[:, 5, d * KR + c:d * KR + c + 1]
                    eng.activation(Q[:, c, :], RA[:, c, :], ACT.Tanh, scale=la).then_inc(s.tanh_exp_done, 1)
                    eng.activation(RA[:, c, :], RA[:, c, :], ACT.Exp, scale=la).then_inc(s.tanh_exp_done, 1)
                for c in range(KR):
                    eng.wait_ge(s.q_ready, d * KR + c + 1)
                    eng.activation(Q[:, c, :], Q[:, c, :], ACT.Sqrt, scale=-1.0).then_inc(s.m_ready, 1)
            eng.wait_ge(s.state_turned, 1)
            eng.copy(hlT[:, :], PS[0:2 * KR, 7, 0:P]).then_inc(s.state_copied, 1)
            norm_out(0)

            def silu(sg_, j):
                eng.wait_ge(sg_.gu_done, j + 1)
                eng.activation(sg, PS[:, 6, 0:F], ACT.Silu).then_inc(sg_.silu_ready, 1)

            def copy_hidden(sg_, j):
                eng.wait_ge(sg_.h_turned, j + 1)
                eng.copy(hT2.rearrange("p f n -> p (f n)"), PS[:, 7, 0:F]).then_inc(sg_.hT_ready, 1)

            def copy_gathered(sg_, j):
                eng.wait_ge(sg_.gathered, 2 * j + 1)
                eng.copy(xg[:, 0:4, :].rearrange("p k n -> p (k n)"), PS[:, 6, :]).then_inc(sg_.xg_act, 1)

            def copy_down(sg_, j):
                eng.wait_ge(sg_.down_done, 2 * j + 1)
                eng.copy(osb[:, 0:512], PS[:, 4, :]).then_inc(sg_.o_act, 1)

            def moe(L):
                n = 2 * L + 1
                norm_in(n)
                eng.wait_ge(s.logits_done, L + 1)
                if L:
                    eng.wait_ge(s.kv_stored, 32)
                eng.activation(scores, PS[:, 4, 0:NS * E].rearrange("p (s e) -> p s e", s=NS), ACT.Sigmoid)\
                   .then_inc(s.scores_ready, 1)
                for b in (1, 3):
                    eng.wait_ge(s.xm_turned, 4 * L + b + 1)
                    eng.copy(xm[:, b // 2, b % 2 * 512:(b % 2 + 1) * 512], PS[:, (5, 6, 7, 5)[b], :])\
                       .then_inc(s.xm_act, 1)
                copy_ggb(n)
                for fc in range(2):
                    eng.wait_ge(s.sh_summed, 2 * L + fc + 1)
                    eng.activation(shg[:, fc, :], PS[:, 4 + 2 * fc, 0:T], ACT.Silu).then_inc(s.sh_silu, 1)
                eng.wait_ge(s.ppT_turned, L + 1)
                act.keep(eng.copy(ppT[0:E, :], PS[0:E, 7, 0:T]))
                eng.copy(combT[0:E, :], PS[0:E, 7, T:2 * T]).then_inc(s.ppT_ready, 1)

                def group(it, last):
                    for i in range(2):
                        j = L * PAIRS + it * 2 + i
                        silu(s, j)
                        copy_hidden(s, j)
                        if not (last and i == 1):
                            copy_gathered(s, j + 1)
                        copy_down(s, j)

                copy_gathered(s, L * PAIRS)
                with eng.Fori(0, PAIRS // 2 - 1) as it:
                    group(it, False)
                group(PAIRS // 2 - 1, True)
                xs = extra[L]
                eng.wait_ge(s.xtable_ready, L + 1)
                count = eng.value_load(xtab[0:1, 32:33], min_val=0, max_val=XITEMS)
                with eng.Fori(0, XITEMS // 2) as i:
                    with eng.If(i * 2 < count):
                        copy_gathered(xs, i)
                        silu(xs, i)
                        copy_hidden(xs, i)
                        copy_down(xs, i)
                norm_out(n)

            moe(0)

            eng.wait_ge(s.x_new, 4)
            eng.dma_start(kv_c[:, 0], a["cache_k"][0, 0].rearrange("t h e -> t (h e)")).then_inc(s.cache_loaded, 16)
            eng.dma_start(kv_c[:, 1], a["cache_v"][0, 0].rearrange("t h e -> t (h e)")).then_inc(s.cache_loaded, 16)
            norm_in(2)
            for j in range(6):
                eng.wait_ge(s.qkv_summed, 2 * j + 1)
                eng.copy(qkv[:, j // 2, 0, j % 2 * 512:(j % 2 + 1) * 512], PS[:, 2 * j % 4, :]).then_inc(s.qkv_act, 1)
            copy_ggb(2)
            for g in range(0, 10, 2):
                eng.wait_ge(s.qk_turned, g + 1)
                eng.copy(TURNS[g][1], PS[:, 4 + g % 4, :].rearrange("p (h t) -> p h t", h=4)).then_inc(s.qkT_act, 1)
            for step in range(NS * H + 2):
                if step < NS * H:
                    j = step
                    eng.wait_ge(s.nm_ready, j + 1)
                    if j >= 2:
                        eng.wait_ge(s.w_ready, j - 1)
                    for comp in range(2):
                        n = P * (j // H + 1)
                        eng.activation(pr[:, j % 2, comp, 0:n], PS[:, 2 * (j % 2) + comp, 0:n], ACT.Exp,
                                       scale=SCALE, bias=sst[:, 0, j, comp:comp + 1],
                                       accum_out=sst[:, 1, j, comp:comp + 1]).then_inc(s.p_ready, 1)
                if 1 <= step <= NS * H:
                    j = step - 1
                    eng.wait_ge(s.wt_turned, j + 1)
                    if j >= 2:
                        eng.wait_ge(s.pv_done, j - 1)
                    n = P * (j // H + 1)
                    eng.copy(wmT[:, j % 2, 0:n], PS[:, 4 + j % 2, 0:n]).then_inc(s.wt_ready, 1)
                if step >= 2:
                    j = step - 2
                    st, h = divmod(j, H)
                    eng.wait_ge(s.o_copied, j + 1)
                    if j:
                        eng.wait_ge(s.o_squared, j)
                    eng.activation(junk[:, 0:P], ot[:, st, h * P:(h + 1) * P], ACT.Square,
                                   accum_out=sst[:, 3, j, 0:1]).then_inc(s.o_squared, 1)
            eng.wait_ge(s.o_squared, 16)
            eng.activation(sst[:, 3, :, 1], sst[:, 3, :, 0], ACT.Sqrt, scale=1.0 / P, bias=epsc)\
               .then_inc(s.o_rms, 1)
            for b in (1, 3):
                st, half = divmod(b, 2)
                eng.wait_ge(s.oT_turned, b + 1)
                eng.activation(oT[:, 4 * half:4 * half + 4, st * P:(st + 1) * P],
                               PS[:, 4 + b, :].rearrange("p (h t) -> p h t", h=4), ACT.Copy,
                               scale=lam[:, 6:7]).then_inc(s.oT_act, 1)
            norm_out(2)
            moe(1)

        @block.vector
        def _(eng):
            dve = Steps(eng, s.dve_step)

            def norm_in(n):
                eng.wait_ge(s.rms_in, n + 1)
                dve.keep(eng.reciprocal(stat[:, 1, :], stat[:, 1, :]))
                dve.settle()
                for st in range(NS):
                    eng.tensor_scalar(junk2[:, st, :], x[:, st, :], stat[:, 1, st:st + 1], None, ALU.mult)\
                       .then_inc(s.xn_ready, 1)
                for b in (0, 2):
                    st, half = divmod(b, 2)
                    eng.wait_ge(s.xT_turned, 4 * n + b + 1)
                    for i in range(4):
                        k = half * 4 + i
                        ins = eng.tensor_scalar(hT[:, k, st * P:(st + 1) * P], PS[:, 4 + b, i * P:(i + 1) * P],
                                                amod[:, n, k, st:st + 1], bmod(n)[:, k, st:st + 1],
                                                ALU.mult, ALU.add)
                    ins.then_inc(s.hT_dve, 1)
                eng.wait_ge(s.xT_turned, 4 * n + 4)
                for b in range(4):
                    for i in range(4):
                        ins = eng.tensor_scalar(diag[:, 4 * b + i, :], ident,
                                                gg[:, n, (b % 2) * 4 + i, b // 2:b // 2 + 1], None, ALU.mult)
                    ins.then_inc(s.diag_ready, 1)

            def residual(n):
                eng.wait_ge(s.rms_out, n + 1)
                dve.keep(eng.reciprocal(stat[:, 3, :], stat[:, 3, :]))
                dve.settle()
                for st in range(NS):
                    dve.keep(eng.scalar_tensor_tensor(out=junk2[:, st, :], in0=Y[:, st, :],
                                                      scalar=stat[:, 3, st:st + 1], in1=ggb[:, st, :],
                                                      op0=ALU.mult, op1=ALU.mult))
                dve.settle()
                for st in range(NS):
                    eng.tensor_tensor(x[:, st, :], x[:, st, :], junk2[:, st, :], ALU.add).then_inc(s.x_new, 1)

            eng.wait_ge(s.vecs_turned, 1)
            for i, (n, at) in enumerate(ROW_TILES):
                ins = eng.tensor_copy(vecs[:, i, 0:n], PS[:, 7, at:at + n])
            ins.then_inc(s.vecs_ready, 1)
            eng.wait_ge(s.vecs_ready, 1)
            dve.keep(eng.tensor_scalar(sp[:, 4, :], neglam, -1.0, None, ALU.mult))
            dve.settle()
            eng.tensor_tensor(sp[:, 0, :], sp[:, 4, :], neglam, ALU.min).then_inc(s.dve_first, 1)
            eng.wait_ge(s.lambda_loaded, 16)
            dve.keep(eng.tensor_tensor(junk2[:, 0, 0:128].rearrange("p (a d) -> p a d", a=2),
                                       lamrow[:, 0:4:2, :], lamrow[:, 1:4:2, :], ALU.mult))
            dve.settle()
            eng.tensor_reduce(lam[:, 0:2], junk2[:, 0, 0:128].rearrange("p (a d) -> p a d", a=2), AX, ALU.add)\
               .then_inc(s.dve_first, 1)
            eng.wait_ge(s.decay_exp, 1)
            dve.keep(eng.tensor_scalar(sp[:, 2, :], sp[:, 1, :], 2.0, None, ALU.add))
            dve.settle()
            dve.keep(eng.reciprocal(sp[:, 2, :], sp[:, 2, :]))
            dve.settle()
            dve.keep(eng.tensor_tensor(sp[:, 1, :], sp[:, 1, :], sp[:, 2, :], ALU.mult))
            dve.settle()
            dve.keep(eng.tensor_tensor(sp[:, 2, :], sp[:, 1, :], sp[:, 1, :], ALU.mult))
            dve.settle()
            dve.keep(eng.tensor_scalar(sp[:, 3, :], sp[:, 2, :], 1.0 / 17, 1.0 / 15, ALU.mult, ALU.add))
            for k in (13, 11, 9, 7, 5, 3, 1):
                dve.settle()
                dve.keep(eng.tensor_tensor(sp[:, 3, :], sp[:, 3, :], sp[:, 2, :], ALU.mult))
                dve.settle()
                dve.keep(eng.tensor_scalar(sp[:, 3, :], sp[:, 3, :], 1.0 / k, None, ALU.add))
            dve.settle()
            dve.keep(eng.scalar_tensor_tensor(out=sp[:, 3, :], in0=sp[:, 3, :], scalar=2.0, in1=sp[:, 1, :],
                                              op0=ALU.mult, op1=ALU.mult))
            dve.keep(eng.tensor_scalar(sp[:, 4, :], sp[:, 4, :], 0.0, None, ALU.max))
            dve.settle()
            dve.keep(eng.tensor_tensor(sp[:, 3, :], sp[:, 3, :], sp[:, 4, :], ALU.add))
            dve.settle()
            eng.tensor_scalar(sp[:, 5, :], sp[:, 3, :], -8.0, None, ALU.mult).then_inc(s.decay_ready, 1)
            eng.wait_ge(s.lam_exp, 1)
            dve.keep(eng.tensor_tensor(lam[:, 5:6], lam[:, 3:4], lam[:, 2:3], ALU.subtract))
            dve.settle()
            eng.tensor_scalar(lam[:, 4:5], lam[:, 5:6], -LAM0, None, ALU.add).then_inc(s.lam_ready, 1)
            eng.tensor_scalar(lam[:, 6:7], vecs[:, 3, 20:21], 1.0 - LAM0, None, ALU.mult).then_inc(s.lam_ready, 1)
            for L in range(2):
                eng.wait_ge(s.mod_done, 8 * (L + 1))
                dve.keep(eng.tensor_tensor(modT[:, L], PS[:, 5 + L, 0:96].rearrange("p (m s) -> p m s", s=NS),
                                           bc(vecs[:, 1, 48 * L:48 * L + 48], 2, NS), ALU.add))
                dve.settle()
                for q in range(2):
                    dve.keep(eng.scalar_tensor_tensor(out=amod[:, 2 * L + q], in0=modT[:, L, 24 * q + 8:24 * q + 16],
                                                      scalar=1.0, in1=bc(gvec(L, 2 * q), 2, NS),
                                                      op0=ALU.add, op1=ALU.mult))
                    dve.keep(eng.tensor_tensor(gg[:, 2 * L + q], modT[:, L, 24 * q + 16:24 * q + 24],
                                               bc(gvec(L, 2 * q + 1), 2, NS), ALU.mult))
                dve.settle()
            eng.tensor_copy(lam[:, 7:8], epsc).then_inc(s.mods_ready, 1)

            norm_in(0)
            dve.keep(eng.memset(xpad[:, :, :, 0:2], 0.0))
            dve.keep(eng.memset(xpad[:, :, :, 130:132], 0.0))
            dve.settle()
            for c in range(KR):
                eng.wait_ge(s.win_done, KR + c + 1)
                eng.tensor_copy(xpad[:, c, :, 2:130], PS[:, (KR + c) % 4, 0:T].rearrange("p (s t) -> p s t", s=NS))\
                   .then_inc(s.xr_ready, 1)
                eng.wait_ge(s.xr_ready, c + 1)
                y = xc[:, c, :].rearrange("p (s t) -> p s t", s=NS)
                dve.keep(eng.tensor_scalar(y, xpad[:, c, :, 0:P], conv_w(0, c), conv_b(c), ALU.mult, ALU.add))
                for t in range(1, 4):
                    dve.settle()
                    ins = eng.scalar_tensor_tensor(out=y, in0=xpad[:, c, :, t:t + P], scalar=conv_w(t, c),
                                                   in1=y, op0=ALU.mult, op1=ALU.add)
                    if t < 3:
                        dve.keep(ins)
                ins.then_inc(s.xc_ready, 1)
            for d in range(2):
                for c in range(KR):
                    eng.wait_ge(s.tanh_exp_done, 2 * (d * KR + c + 1))
                    dve.keep(eng.tensor_tensor(sq[:, c % 2, :], RA[:, c, :], RA[:, c, :], ALU.mult))
                    dve.settle()
                    eng.scalar_tensor_tensor(out=Q[:, c, :], in0=sq[:, c % 2, :], scalar=1.0, in1=Q[:, c, :],
                                             op0=ALU.add, op1=ALU.mult).then_inc(s.q_ready, 1)
                eng.wait_ge(s.ix_ready, d + 1)
                for c in range(KR):
                    eng.wait_ge(s.m_ready, d * KR + c + 1)
                    eng.tensor_tensor(IU[:, c, :], IU[:, c, :], Q[:, c, :], ALU.mult).then_inc(s.u_ready, 1)
                    eng.wait_ge(s.u_ready, d * KR + c + 1)
                    out = (HF, Q)[d]
                    for st in range(NS):
                        cut = slice(st * P, (st + 1) * P)
                        A_, U_, O_ = RA[:, c, cut], IU[:, c, cut], out[:, c, cut]
                        if d:
                            A_, U_, O_ = A_[:, ::-1], U_[:, ::-1], O_[:, ::-1]
                        start = vecs[:, 3, d * KR + c:d * KR + c + 1] if st else 0.0
                        dve.keep(eng.tensor_tensor_scan(O_, A_, U_, start, ALU.mult, ALU.add))
                dve.settle()
                ins = eng.tensor_copy(hl[:, d, :], HF[:, :, P - 1] if d == 0 else Q[:, :, 0])
                ins.then_inc(s.dir_done if d == 0 else s.state_ready, 1)
            for c in range(KR):
                dve.keep(eng.tensor_tensor(HF[:, c, :], HF[:, c, :], Q[:, c, :], ALU.add))
                dve.settle()
                eng.tensor_tensor(gel[:, c, :], gel[:, c, :], HF[:, c, :], ALU.mult).then_inc(s.yT_ready, 1)
            residual(0)

            def one_hots(sg_, item, j, buf):
                eng.tensor_tensor(S[buf].rearrange("p s (e n) -> p s e n", e=2),
                                  bc(bc(iota, 1, 2), 1, NS),
                                  bc(posI[:, bass.ds(item, 2), :].rearrange("p e s -> p s e"), 3, 64),
                                  ALU.is_equal).then_inc(sg_.s_ready, 1)

            def weighted(sg_, item, j, buf):
                eng.wait_ge(sg_.s_ready, j + 1)
                eng.tensor_tensor(Sw.rearrange("p s (e n) -> p s e n", e=2),
                                  S[buf].rearrange("p s (e n) -> p s e n", e=2),
                                  bc(comI[:, bass.ds(item, 2), :].rearrange("p e s -> p s e"), 3, 64),
                                  ALU.mult).then_inc(sg_.sw_ready, 1)

            def hidden(sg_, j):
                eng.wait_ge(sg_.silu_ready, j + 1)
                eng.tensor_tensor(hE, sg, PS[:, 6, F:2 * F], ALU.mult).then_inc(sg_.h_ready, 1)

            def copy_gathered(sg_, j):
                eng.wait_ge(sg_.gathered, 2 * j + 2)
                eng.tensor_copy(xg[:, 4:8, :].rearrange("p k n -> p (k n)"), PS[:, 7, :]).then_inc(sg_.xg_dve, 1)

            def copy_down(sg_, j):
                eng.wait_ge(sg_.down_done, 2 * j + 2)
                eng.tensor_copy(osb[:, 512:1024], PS[:, 5, :]).then_inc(sg_.o_dve, 1)

            def copy_weights(sg_, j):
                eng.wait_ge(sg_.wT_turned, j + 1)
                eng.tensor_copy(wT, PS[:, 7, 256:512]).then_inc(sg_.wT_ready, 1)

            def route(L):
                eng.wait_ge(s.scores_ready, L + 1)
                eng.wait_ge(s.bias_loaded, 16)
                dve.keep(eng.tensor_tensor(sel, scores, bc(bias[:, L, :], 1, NS), ALU.add))
                dve.settle()
                for st in range(NS):
                    for g in range(NG):
                        dve.keep(eng.max(gtop[:, st, g, :], sel[:, st, g * 8:(g + 1) * 8]))
                dve.settle()
                dve.keep(eng.tensor_tensor(gsc, gtop[:, :, :, 0], gtop[:, :, :, 1], ALU.add))
                dve.settle()
                for st in range(NS):
                    dve.keep(eng.max(gm8[:, st, :], gsc[:, st, :]))
                dve.settle()
                for st in range(NS):
                    dve.keep(eng.max_index(idx[:, st, :], gm8[:, st, :], gsc[:, st, :]))
                dve.settle()
                dve.keep(eng.tensor_copy(idxf, idx[:, :, :]))
                dve.settle()
                for st in range(NS):
                    dve.keep(eng.tensor_tensor(eq[:, st], bc(idxf[:, st, 0:TOPG], 1, NG), bc(iota[:, 0:NG], 2, TOPG),
                                               ALU.is_equal))
                dve.settle()
                dve.keep(eng.tensor_reduce(gmask, eq, AX, ALU.max))
                dve.settle()
                grouped = [v.rearrange("p s (g e) -> p (s g) e", g=NG) for v in (masked, sel)]
                gm = gmask.rearrange("p s g -> p (s g)")
                dve.keep(eng.tensor_tensor(grouped[0], grouped[1], bc(gm, 2, 8), ALU.mult))
                dve.keep(eng.tensor_scalar(gsc, gmask, -1.0, BIG, ALU.add, ALU.mult))
                dve.settle()
                dve.keep(eng.tensor_tensor(grouped[0], grouped[0], bc(gsc.rearrange("p s g -> p (s g)"), 2, 8),
                                           ALU.add))
                dve.settle()
                for st in range(NS):
                    dve.keep(eng.max(gm8[:, st, :], masked[:, st, :]))
                dve.settle()
                for st in range(NS):
                    dve.keep(eng.match_replace(rep[:, st, :], gm8[:, st, :], masked[:, st, :], -1.1 * BIG))
                dve.settle()
                eng.tensor_tensor(mask, rep, masked, ALU.is_lt).then_inc(s.mask_ready, 1)
                eng.wait_ge(s.mask_ready, L + 1)
                dve.keep(eng.tensor_tensor(comb, scores, mask, ALU.mult))
                dve.settle()
                dve.keep(eng.tensor_reduce(wsum[:, :, 0], comb, AX, ALU.add))
                dve.settle()
                dve.keep(eng.reciprocal(wsum[:, :, 1], wsum[:, :, 0]))
                dve.settle()
                dve.keep(eng.scalar_tensor_tensor(out=comb, in0=comb, scalar=ROUTED, in1=bc(wsum[:, :, 1], 2, E),
                                                  op0=ALU.mult, op1=ALU.mult))

            def moe(L):
                n = 2 * L + 1
                norm_in(n)
                if L:
                    eng.wait_ge(s.kv_stored, 32)
                for b in (0, 2):
                    eng.wait_ge(s.xm_turned, 4 * L + b + 1)
                    eng.tensor_copy(xm[:, b // 2, b % 2 * 512:(b % 2 + 1) * 512], PS[:, (5, 6, 7, 5)[b], :])\
                       .then_inc(s.xm_dve, 1)
                route(L)
                for fc in range(2):
                    eng.wait_ge(s.sh_silu, 2 * L + fc + 1)
                    eng.tensor_tensor(shh[:, fc, :], shg[:, fc, :], PS[:, 5 + 2 * fc, 0:T], ALU.mult)\
                       .then_inc(s.sh_h, 1)
                eng.wait_ge(s.ranks_done, L + 1)
                dve.settle()
                dve.keep(eng.tensor_tensor(pp, PS[:, 4, 0:NS * E].rearrange("p (s e) -> p s e", s=NS), mask,
                                           ALU.mult))
                dve.settle()
                dve.keep(eng.tensor_copy(comI[:, 0:E, :].rearrange("p e s -> p s e"), comb))
                eng.tensor_scalar(posI[:, 0:E, :].rearrange("p e s -> p s e"), pp, -1.0, None, ALU.add)\
                   .then_inc(s.pos_ready, 1)
                eng.wait_ge(s.counts_done, L + 1)
                for i in range(3):
                    dve.keep(eng.tensor_scalar(nb[0:E, 0, i:i + 1], PS[0:E, 5, 0:1], float(SLOTS * (i + 1)), None,
                                               ALU.is_gt))
                dve.settle()
                dve.keep(eng.tensor_tensor(nb[0:E, 0, 3:4], nb[0:E, 0, 0:1], nb[0:E, 0, 1:2], ALU.add))
                dve.settle()
                eng.tensor_tensor(nb[0:E, 0, 4:5], nb[0:E, 0, 3:4], nb[0:E, 0, 2:3], ALU.add).then_inc(s.nb_ready, 1)
                eng.wait_ge(s.hi_done, L + 1)
                eng.wait_ge(s.nb_ready, L + 1)
                dve.keep(eng.tensor_copy(nb[0:E, 0, 6:7], PS[0:E, 6, 0:1]))
                dve.keep(eng.tensor_copy(xtab[0:1, 32:33], PS[0:1, 6, 8:9]))
                dve.settle()
                dve.keep(eng.tensor_tensor(nb[0:E, 0, 5:6], nb[0:E, 0, 6:7], nb[0:E, 0, 4:5], ALU.subtract))
                dve.settle()
                dve.keep(eng.tensor_scalar(M[0:E, :], iota[0:E, 0:32], nb[0:E, 0, 6:7], None, ALU.is_lt))
                dve.keep(eng.tensor_scalar(bM[0:E, :], iota[0:E, 0:32], nb[0:E, 0, 5:6], None, ALU.is_lt))
                dve.settle()
                dve.keep(eng.tensor_tensor(M[0:E, :], M[0:E, :], bM[0:E, :], ALU.subtract))
                dve.settle()
                dve.keep(eng.tensor_scalar(bM[0:E, :], iota[0:E, 0:32], nb[0:E, 0, 5:6], 1.0, ALU.subtract, ALU.add))
                dve.settle()
                eng.scalar_tensor_tensor(out=bM[0:E, :], in0=bM[0:E, :], scalar=-float(SLOTS), in1=M[0:E, :],
                                         op0=ALU.mult, op1=ALU.mult).then_inc(s.m_cols_ready, 1)
                eng.wait_ge(s.xtable_done, L + 1)
                dve.keep(eng.tensor_copy(xtab[0:1, 0:32], PS[0:1, 6, 16:48]))
                dve.keep(eng.tensor_scalar(posI[:, E:ITEMS, :].rearrange("p e s -> p s e"),
                                           PS[:, 5, 0:64].rearrange("p (s x) -> p s x", s=NS), -1.0, None, ALU.add))
                eng.tensor_copy(comI[:, E:ITEMS, :].rearrange("p e s -> p s e"),
                                PS[:, 5, 64:128].rearrange("p (s x) -> p s x", s=NS)).then_inc(s.xtable_ready, 1)
                eng.wait_ge(s.xtable_ready, L + 1)
                eng.wait_ge(s.pos_ready, L + 1)
                dve.settle()

                def group(it, last):
                    for i in range(2):
                        j = L * PAIRS + it * 2 + i
                        item = it * 4 + 2 * i
                        if not (last and i == 1):
                            one_hots(s, item + 2, j + 1, (i + 1) % 2)
                        weighted(s, item, j, i)
                        hidden(s, j)
                        if not (last and i == 1):
                            copy_gathered(s, j + 1)
                        copy_down(s, j)
                        copy_weights(s, j)

                one_hots(s, 0, L * PAIRS, 0)
                copy_gathered(s, L * PAIRS)
                with eng.Fori(0, PAIRS // 2 - 1) as it:
                    group(it, False)
                group(PAIRS // 2 - 1, True)
                xs = extra[L]
                eng.wait_ge(s.scattered, 2 * (L + 1) * PAIRS)
                count = eng.value_load(xtab[0:1, 32:33], min_val=0, max_val=XITEMS)
                with eng.Fori(0, XITEMS // 2) as i:
                    with eng.If(i * 2 < count):
                        one_hots(xs, i * 2 + E, i, 0)
                        weighted(xs, i * 2 + E, i, 0)
                        copy_gathered(xs, i)
                        hidden(xs, i)
                        copy_down(xs, i)
                        copy_weights(xs, i)
                residual(n)

            moe(0)

            norm_in(2)
            for j in range(6):
                eng.wait_ge(s.qkv_summed, 2 * j + 2)
                eng.tensor_copy(qkv[:, j // 2, 1, j % 2 * 512:(j % 2 + 1) * 512], PS[:, (2 * j + 1) % 4, :])\
                   .then_inc(s.qkv_dve, 1)
            for g in (1, 3, 5):
                eng.wait_ge(s.qk_turned, g + 1)
                eng.tensor_copy(TURNS[g][1], PS[:, 4 + g % 4, :].rearrange("p (h t) -> p h t", h=4))\
                   .then_inc(s.qkT_dve, 1)
            eng.wait_ge(s.qkv_dve, 6)
            for w in range(2):
                src = qkv[:, w, 1].rearrange("p (h a b j) -> p h a b j", h=2 * H, a=2, b=2)
                rot = rope[:, w].rearrange("p (h a b j) -> p h a b j", h=2 * H, a=2, b=2)
                sn = con[:, C_SIN:C_SIN + HD].rearrange("p (a b j) -> p a b j", a=2, b=2)
                for b in range(2):
                    dve.keep(eng.tensor_tensor(rot[:, :, :, b, :], src[:, :, :, 1 - b, :],
                                               bc(sn[:, :, b, :], 1, 2 * H), ALU.mult))
            dve.settle()
            for w in range(2):
                src = qkv[:, w, 1].rearrange("p (h d) -> p h d", h=2 * H)
                dve.keep(eng.tensor_tensor(src, src, bc(con[:, C_COS:C_COS + HD], 1, 2 * H), ALU.mult))
            dve.settle()
            for w in range(2):
                ins = eng.tensor_tensor(qkv[:, w, 1], qkv[:, w, 1], rope[:, w], ALU.add)
                if w == 0:
                    dve.keep(ins)
            ins.then_inc(s.roped, 1)
            for g in (7, 9):
                eng.wait_ge(s.qk_turned, g + 1)
                eng.tensor_copy(TURNS[g][1], PS[:, 4 + g % 4, :].rearrange("p (h t) -> p h t", h=4))\
                   .then_inc(s.qkT_dve, 1)
            eng.wait_ge(s.lam_ready, 2)
            for step in range(NS * H + 2):
                if step < NS * H:
                    j = step
                    eng.wait_ge(s.sc_done, j + 1)
                    n = P * (j // H + 1)
                    b0 = 2 * (j % 2)
                    dve.keep(eng.tensor_reduce(sst[:, 0, j, :], PS[:, b0:b0 + 2, 0:n], AX, ALU.max))
                    dve.settle()
                    eng.tensor_scalar(sst[:, 0, j, :], sst[:, 0, j, :], -SCALE, None, ALU.mult)\
                       .then_inc(s.nm_ready, 1)
                if 1 <= step <= NS * H:
                    j = step - 1
                    n = P * (j // H + 1)
                    eng.wait_ge(s.p_ready, 2 * (j + 1))
                    dve.keep(eng.reciprocal(sst[:, 2, j, :], sst[:, 1, j, :]))
                    dve.settle()
                    dve.keep(eng.tensor_scalar(pr[:, j % 2, 1, 0:n], pr[:, j % 2, 1, 0:n], sst[:, 2, j, 1:2],
                                               lam[:, 4:5], ALU.mult, ALU.mult))
                    dve.settle()
                    if j >= 2:
                        eng.wait_ge(s.wt_turned, j - 1)
                    eng.scalar_tensor_tensor(out=wmix[:, j % 2, 0:n], in0=pr[:, j % 2, 0, 0:n],
                                             scalar=sst[:, 2, j, 0:1], in1=pr[:, j % 2, 1, 0:n],
                                             op0=ALU.mult, op1=ALU.add).then_inc(s.w_ready, 1)
                if step >= 2:
                    j = step - 2
                    st, h = divmod(j, H)
                    eng.wait_ge(s.pv_done, j + 1)
                    eng.tensor_copy(ot[:, st, h * P:(h + 1) * P], PS[:, 6 + j % 2, 0:P]).then_inc(s.o_copied, 1)
            eng.wait_ge(s.o_rms, 1)
            dve.keep(eng.reciprocal(sst[:, 3, :, 1], sst[:, 3, :, 1]))
            eng.wait_ge(s.o_copied, 16)
            dve.settle()
            v = ot.rearrange("p s (h e) -> p (s h) e", h=H)
            eng.tensor_tensor(v, v, bc(sst[:, 3, :, 1], 2, P), ALU.mult).then_inc(s.o_normed, 1)
            for b in (0, 2):
                st, half = divmod(b, 2)
                eng.wait_ge(s.oT_turned, b + 1)
                eng.tensor_scalar(oT[:, 4 * half:4 * half + 4, st * P:(st + 1) * P],
                                  PS[:, 4 + b, :].rearrange("p (h t) -> p h t", h=4), lam[:, 6:7], None,
                                  ALU.mult).then_inc(s.oT_dve, 1)
            residual(2)
            moe(1)


_INS = ["x_prompt", "x_sample", "c", "state_lru", "cache_k", "cache_v", "c_ctx", "mod_w", "mod_b", "norm_g",
        "lru_w_in", "lru_conv_w", "lru_conv_b", "lru_gate_w", "lru_gate_b", "lru_lambda", "lru_w_out",
        "attn_w_qkv", "attn_lambda", "attn_subln", "attn_w_o", "moe_router", "moe_router_bias", "moe_w_gate",
        "moe_w_up", "moe_w_down", "shared_w_gate", "shared_w_up", "shared_w_down"]
_OUTS = [(1, P, D), (1, P, D), (1, 1, 2, R), (1, 1, P, H, 2 * HD), (1, 1, P, H, 2 * HD)]


def kernel(**inputs):
    import concourse.bacc as bacc
    from concourse.bass_utils import run_bass_kernel_spmd

    nc = bacc.Bacc("TRN2", target_bir_lowering=False, num_devices=1)
    arrays = {name: np.ascontiguousarray(inputs[name]) for name in _INS}
    arrays["constants"] = constants()
    a = {name: nc.dram_tensor(f"in_{name}", v.shape, F32, kind="ExternalInput").ap() for name, v in arrays.items()}
    outs = [nc.dram_tensor(f"out_{i}", shape, F32, kind="ExternalOutput").ap() for i, shape in enumerate(_OUTS)]
    trunk(nc, a, outs)
    r = run_bass_kernel_spmd(nc, [{f"in_{name}": v for name, v in arrays.items()}], core_ids=[0])
    return tuple(r.results[0][f"out_{i}"] for i in range(len(_OUTS)))
```

```python
import math
from collections import namedtuple
from contextlib import ExitStack

import numpy as np

import concourse.bass as bass
from concourse import mybir

F32 = mybir.dt.float32
I32 = mybir.dt.int32
U32 = mybir.dt.uint32
BF16 = mybir.dt.bfloat16
ALU = mybir.AluOpType
ACT = mybir.ActivationFunctionType
AX = mybir.AxisListType.X

P = 128
NS = 2
T = NS * P
D = 1024
KD = D // P
R = 1280
KR = R // P
BLK = 80
HALF = 640
H = 8
HD = 64
E = 64
NG = 8
TOPG = 4
F = 256
SLOTS = 64
XITEMS = T * 8 // SLOTS
ITEMS = E + XITEMS
PAIRS = E // 2
EPS = 1e-6
ROUTED = 2.5
BIG = 3.0e38
LAM0 = 0.8 - 0.6 * math.exp(-0.3)
SCALE = HD ** -0.5
RING = 4
SLOT = 6144

MB = 768

N_MOD = (1, 2, 3, 5, 6, 8, 9, 11, 12, 14, 15, 20, 21, 24, 25, 28)
N_WIN = (4, 7, 10, 13)
N_GATE = 16
N_WOUT = (29, 32)
N_ROUTER = (30, 110)
N_EXPERT = (36, 112)
N_QKV, N_WO = 100, 106
N_LEFT_OUT = (0, 22, 23, 26, 27, 31, 33, 34, 35, 111)
EARLY, AHEAD = 3, 11

G_START = [0, 0, 128, 256, 384]
G_END = [256, 384, 512, 640, 640]
G_OFF = [0, 256, 640, 1024, 1408]
G_HALF = 1664
GATE_BANKS = (0, 1, 2, 3, 7)
XM_BANKS = (5, 6, 2, 3)
G_INPUTS = [[k for k in range(5) if G_START[k] <= c * P < G_END[k]] for c in range(5)]

C_ID, C_TRI, C_ONE, C_IOTA, C_E, C_EPS, C_COS, C_SIN = 0, 128, 256, 384, 448, 449, 450, 514
C_SEL = 578
C_FOLD = 580
C_N = 644


def constants():
    c = np.zeros((P, C_N), np.float32)
    c[:, C_ID:C_ID + P] = np.eye(P)
    c[:, C_TRI:C_TRI + P] = np.triu(np.ones((P, P)))
    c[:, C_ONE:C_ONE + P] = 1.0
    c[:, C_IOTA:C_IOTA + 64] = np.arange(64)
    c[:, C_E] = np.arange(P)
    c[:, C_EPS] = EPS
    c[:, C_FOLD:C_FOLD + E] = np.tile(np.eye(E), (2, 1))
    for stream in range(NS):
        c[stream::32, C_SEL + stream] = 1.0
    pairs = HD // 4
    freqs = (10000.0 ** (-np.arange(pairs, dtype=np.float32) / pairs)).astype(np.float32)
    t = np.arange(P)
    ar = (t // 64).astype(np.float32)[:, None] * freqs
    ac = (t % 64).astype(np.float32)[:, None] * freqs
    c[:, C_COS:C_COS + HD] = np.concatenate([np.cos(ar), np.cos(ar), np.cos(ac), np.cos(ac)], 1)
    c[:, C_SIN:C_SIN + HD] = np.concatenate([-np.sin(ar), np.sin(ar), -np.sin(ac), np.sin(ac)], 1)
    return c


SEMAPHORES = """
shared_loaded consts_loaded rows_loaded x_loaded vectors_loaded cache_loaded
dve_first slot0_loaded slot1_loaded slot2_loaded slot3_loaded
down0_loaded down1_loaded down2_loaded down3_loaded
gate0_loaded gate1_loaded gate2_loaded gate3_loaded gate_zeroed
vecs_turned vecs_ready cond_ready mod_summed mod_act mod_dve mod_done mods_ready dve_step act_step
rms_in xn_ready xT_turned hT_dve hT_act diag_ready ggb_summed ggb_ready
win_done gelu_ready xr_ready xc_ready gate_summed gates_ready tanh_exp_done q_ready m_ready
ix_ready u_ready exps_done decay_ready yT_ready wout_half mixer_done
state_ready state_turned state_copied state_stored rms_out x_new
logits_done scores_ready xm_turned xm_dve xm_act xm_pool sh_summed sh_silu sh_h router_summed router_copied
mask_ready ranks_done pos_ready nb_ready hi_done m_cols_ready ppT_turned ppT_ready
xtable_done xtable_ready
lam_ready qkv_summed qkv_act qkv_dve roped qk_turned qkT_act qkT_dve
sc_done nm_ready p_ready w_ready wt_turned wt_ready pv_done o_copied o_squared o_rms o_normed oT_turned
oT_act oT_dve wo_done kv_stored outputs_stored y_done
""".split()
PAIR_SEMAPHORES = """
s_ready sw_ready gathered xg_act xg_dve gu_done silu_ready h_ready h_turned hT_ready down_done
o_act o_dve wT_turned wT_ready scattered
""".split()
SEMAPHORES += PAIR_SEMAPHORES + [f"x{L}_{n}" for L in (0, 1) for n in ["loaded"] + PAIR_SEMAPHORES]


class Steps:

    def __init__(self, eng, sem):
        self.eng, self.sem, self.n = eng, sem, 0

    def keep(self, ins):
        ins.then_inc(self.sem, 1)
        self.n += 1

    def settle(self):
        self.eng.wait_ge(self.sem, self.n)


def slot_value(n):
    expert = [e for n0 in N_EXPERT for e in range(n0, n0 + E)]
    silent = N_LEFT_OUT + tuple(range(N_GATE, N_GATE + RING))
    return sum(0 if m in silent else 32 if m in expert else 48 for m in range(n % RING, n + 1, RING))


def trunk(nc, a, outs):
    y_prompt, y_sample, new_state, new_k, new_v = outs
    ctx = ExitStack()
    with ctx:
        def sb(name, shape, dt=F32):
            return ctx.enter_context(nc.sbuf_tensor(name, shape, dt))

        sem = {name: ctx.enter_context(nc.semaphore(name)) for name in SEMAPHORES}
        s = namedtuple("Signals", SEMAPHORES)(**sem)
        extra = [namedtuple("Extra", ["loaded"] + PAIR_SEMAPHORES)(
            *[sem[f"x{L}_{n}"] for n in ["loaded"] + PAIR_SEMAPHORES]) for L in (0, 1)]

        ring = sb("ring", [P, RING, SLOT])
        con = sb("con", [P, C_N])
        x = sb("x", [P, NS, D])
        hT = sb("hT", [P, KD, T])
        ggb = sb("ggb", [P, NS, D])
        diag = sb("diag", [P, 16, P])
        junk = sb("junk", [P, D])
        rows = sb("rows", [P, 4, P])
        vecs = sb("vecs", [P, 4, P])
        condT = sb("condT", [P, KD, 32])
        modT = sb("modT", [P, 2, 48, NS])
        amod = sb("amod", [P, 4, KD, NS])
        gg = sb("gg", [P, 4, KD, NS])
        stat = sb("stat", [P, 4, NS])
        bias = sb("bias", [P, 2, E])
        lamrow = sb("lamrow", [P, 4, HD])
        lam = sb("lam", [P, 8])
        W = sb("W", [P, 15440])
        PS = ctx.enter_context(nc.psum_tensor("PS", [P, 8, 512], F32))

        ident, tri, ones = con[:, C_ID:C_ID + P], con[:, C_TRI:C_TRI + P], con[:, C_ONE:C_ONE + P]
        iota, ecol, epsc = con[:, C_IOTA:C_IOTA + 64], con[:, C_E:C_E + 1], con[:, C_EPS:C_EPS + 1]
        Y = PS[:, 0:4, :].rearrange("p (s h) n -> p s (h n)", s=NS)

        class Carve:

            def __init__(self):
                self.at = 0

            def __call__(self, *shape):
                n = math.prod(shape)
                v = W[:, self.at:self.at + n]
                self.at += n
                assert self.at <= 15440
                if len(shape) == 2:
                    v = v.rearrange("p (a b) -> p a b", a=shape[0])
                if len(shape) == 3:
                    v = v.rearrange("p (a b c) -> p a b c", a=shape[0], b=shape[1])
                return v

        c = Carve()
        gel, xc = c(KR, T), c(KR, T)
        xpad_flat = c(KR * NS * 132)
        xpad = xpad_flat.rearrange("p (c s t) -> p c s t", c=KR, s=NS)
        Q = xpad_flat[:, 0:KR * T].rearrange("p (c t) -> p c t", c=KR)
        mrow_early = W[:, c.at:c.at + EARLY * MB].rearrange("p (b h n) -> p b h n", b=EARLY, h=2)
        RA, IU, HF = c(KR, T), c(KR, T), c(KR, T)
        RAs = [RA, ring[:, 2, 2 * G_HALF:2 * G_HALF + KR * T].rearrange("p (c t) -> p c t", c=KR)]
        IUs = [IU, ring[:, 3, 2 * G_HALF:2 * G_HALF + KR * T].rearrange("p (c t) -> p c t", c=KR)]
        Qs = [[Q[:, k, :] for k in range(KR)],
              [hT[:, k, :] for k in range(KD)] + [junk[:, k * T:(k + 1) * T] for k in range(KR - KD)]]
        sq = sb("sq", [P, 2, T])
        sp = sb("sp", [P, 6, 2 * KR])
        hl = sb("hl", [P, 2, KR])
        hlT = sb("hlT", [2 * KR, P])
        c = Carve()
        x32 = W[:, NS * D:2 * NS * D]
        parts = [junk[:, :].bitcast(BF16), c(D).bitcast(BF16), c(D).bitcast(BF16)]
        xg, hE, hT2, osb = c(KD, P), c(F), c(2, P), c(D)
        S = [c(P).bitcast(BF16).rearrange("p (s n) -> p s n", s=NS) for _ in range(2)]
        Sw, wT = c(NS, P), c(T)
        posI, comI = c(ITEMS, NS), c(ITEMS, NS)
        shg, shh = c(2, T), c(2, T)
        scores, sel, masked, rep, mask, comb, pp = (c(NS, E) for _ in range(7))
        gtop = c(NS, NG, 8)
        gsc, gm8, idxf, gmask = c(NS, NG), c(NS, 8), c(NS, 8), c(NS, NG)
        eq = c(NS, NG, TOPG)
        wsum = c(NS, 2)
        nb = c(1, 8)
        M, bM = c(32), c(32)
        ppT, combT = c(T), c(T)
        sg = c(F)
        logitsT = sg
        shared_w = c(SLOT)
        idx = sb("idx", [P, NS, 8], U32)
        xtab = sb("xtab", [1, 64], I32)
        c = Carve()
        qkv = c(3, NS, D)
        kv_c = c(2, D)
        qT, kT = c(H, NS, P), c(H, 3, P)
        ot = qkv[:, 0]
        oT = hT
        rope = W[:, c.at:c.at + 2 * D].rearrange("p (w n) -> p w n", w=2)
        pr = c(2, 4, T)
        sst = sb("sst", [P, 5, 16, 2])

        def as_rows(v):
            return v.rearrange("(k p) -> k p", p=P)

        ROW_SOURCES = [
            (0, 0, 64, a["norm_g"].rearrange("i j (k p) -> (i j k) p", p=P)),
            (0, 64, KD, as_rows(a["c_ctx"])), (0, 72, KD, as_rows(a["c"][0])),
            (1, 0, 96, a["mod_b"].rearrange("i (m p) -> (i m) p", p=P)),
            (2, 0, 4 * KR, a["lru_conv_w"][0].rearrange("j (k p) -> (j k) p", p=P)),
            (2, 40, KR, as_rows(a["lru_conv_b"][0])),
            (2, 50, 4 * KR, a["lru_gate_b"][0].rearrange("d g (k p) -> (d g k) p", p=P)),
            (2, 90, 2 * KR, a["lru_lambda"][0].rearrange("d (k p) -> (d k) p", p=P)),
            (3, 0, 2 * KR, a["state_lru"][0, 0].rearrange("d (k p) -> (d k) p", p=P)),
            (3, 20, 1, a["attn_subln"])]
        ROW_LOADS = len(ROW_SOURCES)
        ROW_TILES = [(80, 0), (96, 80), (110, 176), (21, 286)]
        GATE_DMAS = 12

        def conv_w(t, c):
            return vecs[:, 2, t * KR + c:t * KR + c + 1]

        def conv_b(c):
            return vecs[:, 2, 40 + c:41 + c]

        def gate_bias(dg, c):
            return vecs[:, 2, 50 + dg * KR + c:51 + dg * KR + c]

        neglam = vecs[:, 2, 90:110]

        def bmod(n):
            return modT[:, n // 2, 24 * (n % 2):24 * (n % 2) + 8]

        junk2 = diag[:, :, :].rearrange("p (s k) n -> p s (k n)", s=NS)
        mrow_late = diag[:, 0:12, :].rearrange("p k n -> p (k n)").rearrange("p (b h n) -> p b h n", b=2, h=2)
        wmix = diag[:, 0:8, :].rearrange("p (u k) n -> p u (k n)", u=2)
        wmT = diag[:, 8:16, :].rearrange("p (u k) n -> p u (k n)", u=2)
        TURNS = []
        for st, dst in ((0, 2), (None, 0), (1, 1)):
            for half in range(2):
                cols, hs = slice(half * 512, (half + 1) * 512), slice(half * 4, half * 4 + 4)
                if st is not None:
                    TURNS.append((qkv[:, 0, st, cols], qT[:, hs, st, :]))
                TURNS.append(((qkv[:, 1, st] if st is not None else kv_c[:, 0])[:, cols], kT[:, hs, dst, :]))

        def slot(n):
            return ring[:, n % RING]

        def loaded(eng, n):
            eng.wait_ge(sem[f"slot{n % RING}_loaded"], slot_value(n))

        def used(n):
            return (s.win_done, 5 * (N_WIN.index(n) + 1)) if n in N_WIN else (s.mod_summed, N_MOD.index(n) + 1)

        def mod_bank(m):
            return 2 * (m % 2) if m < EARLY else 4

        def mod_rows(m):
            return mrow_early[:, m] if m < EARLY else mrow_late[:, m % 2]

        MOD_DVE = [0, 1, 2, 3, 4, 5, 6, 11, 12, 13, 14]
        MOD_ACT = [0, 1, 2, 7, 8, 9, 10, 15]

        def mod_copied(eng, m):
            if m in MOD_DVE:
                eng.wait_ge(s.mod_dve, MOD_DVE.index(m) + 1)
            if m in MOD_ACT:
                eng.wait_ge(s.mod_act, MOD_ACT.index(m) + 1)

        def mod_place_free(eng, m):
            if m == EARLY:
                eng.wait_ge(s.xT_turned, 4)
            if m >= EARLY + 2:
                eng.wait_ge(s.mod_done, m - 1)

        def gvec(i, j):
            return vecs[:, 0, (i * 4 + j) * KD:(i * 4 + j + 1) * KD]

        def bc(ap, axis, n):
            v = ap.unsqueeze(axis)
            shape = list(v.shape)
            shape[axis] = n
            return v.to_broadcast(shape)

        def ring_view(n, k, width):
            return slot(n)[:, 0:k * width].rearrange("p (k n) -> p k n", k=k)

        def extra_pairs(eng, count, body):
            with eng.If(count > 0):
                body(0)
                with eng.If(count > 2):
                    with eng.Fori(1, XITEMS // 2) as i:
                        with eng.If(i * 2 < count):
                            body(i)

        block = ctx.enter_context(nc.Block())

        @block.sync
        def _(eng):
            def load_rows(n, src, k, width):
                v = ring_view(n, k, width)
                done = sem[f"slot{n % RING}_loaded"]
                if k == 2:
                    pieces = [(slice(0, 1), slice(0, width)), (slice(1, 2), slice(0, width // 2)),
                              (slice(1, 2), slice(width // 2, width))]
                else:
                    cut = {8: (0, 3, 6, 8), 5: (0, 2, 4, 5)}[k]
                    pieces = [(slice(p, q), slice(0, width)) for p, q in zip(cut, cut[1:])]
                for rows_, cols in pieces:
                    eng.dma_start(v[:, rows_, cols], src[:, rows_, cols]).then_inc(done, 16)

            def load_gate_up(place, gate, up, done):
                v = place[:, 0:4096].rearrange("p (k m f) -> p k m f", k=KD, m=2)
                for i, w in enumerate((gate, up)):
                    eng.dma_start(v[:, :, i, :], w.rearrange("(k p) f -> p k f", p=P)).then_inc(done, 16)

            def load_down(place, down, done):
                eng.dma_start(place[:, 4096:6144].rearrange("p (c n) -> p c n", c=2),
                              down.rearrange("(c p) n -> p c n", p=P)).then_inc(done, 16)

            def slot_sem(n):
                return sem[f"slot{n % RING}_loaded"]

            def moe_loads(L, free_router, free_shared, free_first):
                eng.wait_ge(*free_router)
                load_rows(N_ROUTER[L], a["moe_router"][L].rearrange("(k p) n -> p k n", p=P), KD, E)
                eng.wait_ge(*free_shared)
                load_gate_up(shared_w, a["shared_w_gate"][L], a["shared_w_up"][L], s.shared_loaded)
                load_down(shared_w, a["shared_w_down"][L], s.shared_loaded)
                for e in (3, 1, 0, 2) if L == 0 else (3, 0, 1, 2):
                    eng.wait_ge(*free_first[e])
                    load_gate_up(ring[:, e], a["moe_w_gate"][L, e], a["moe_w_up"][L, e], slot_sem(e))
                    load_down(ring[:, e], a["moe_w_down"][L, e], sem[f"down{e}_loaded"])
                with eng.Fori(1, E // RING) as it:
                    for i in range(2):
                        eng.wait_ge(s.gu_done, it * 2 + (L * PAIRS + i - 1))
                        for q in (2 * i, 2 * i + 1):
                            load_gate_up(ring[:, q], a["moe_w_gate"][L, it * RING + q], a["moe_w_up"][L, it * RING + q],
                                         slot_sem(q))
                        eng.wait_ge(s.down_done, it * 4 + 2 * (L * PAIRS + i - 1))
                        for q in (2 * i, 2 * i + 1):
                            load_down(ring[:, q], a["moe_w_down"][L, it * RING + q], sem[f"down{q}_loaded"])

            def extra_loads(L):
                xs = extra[L]
                eng.wait_ge(s.down_done, 2 * ((L + 1) * PAIRS - 1))
                eng.wait_ge(s.xtable_ready, L + 1)
                count = eng.value_load(xtab[0:1, 32:33], min_val=0, max_val=XITEMS)

                def load_pair(i):
                    if not isinstance(i, int):
                        eng.wait_ge(xs.down_done, i * 2)
                    for q in range(2):
                        e = eng.value_load(xtab[0:1, bass.ds(i * 2 + q, 1)], min_val=0, max_val=E - 1)
                        load_gate_up(ring[:, q], a["moe_w_gate"][L, e], a["moe_w_up"][L, e], xs.loaded)
                        load_down(ring[:, q], a["moe_w_down"][L, e], xs.loaded)

                extra_pairs(eng, count, load_pair)

            def load_mod(m):
                L, j = divmod(m, 8)
                load_rows(N_MOD[m], a["mod_w"][L].rearrange("(k p) n -> p k n", p=P)
                          [:, :, j * MB:(j + 1) * MB], KD, MB)

            eng.wait_ge(s.consts_loaded, 16)
            eng.wait_ge(s.rows_loaded, 16 * ROW_LOADS)
            for n in range(1, N_GATE):
                if n > RING:
                    eng.wait_ge(*used(n - RING))
                if n in N_WIN:
                    j = N_WIN.index(n)
                    load_rows(n, a["lru_w_in"][0].rearrange("(k p) n -> p k n", p=P)
                              [:, :, j * HALF:(j + 1) * HALF], KD, HALF)
                else:
                    load_mod(N_MOD.index(n))
            for j in range(4):
                g, d = divmod(j, 2)
                eng.wait_ge(s.gate_zeroed, j + 1)
                store = ring[:, j, 0:2 * G_HALF].rearrange("p (h n) -> p h n", h=2)
                src = a["lru_gate_w"][0, d, g].rearrange("(h b) i j -> b i h j", h=2)
                for b in range(8):
                    r = b * BLK
                    while r < (b + 1) * BLK:
                        k = r // P
                        end = min((k + 1) * P, (b + 1) * BLK)
                        col = G_OFF[k] + b * BLK - G_START[k]
                        eng.dma_start(store[r - k * P:end - k * P, :, col:col + BLK],
                                      src[b, r - b * BLK:end - b * BLK]).then_inc(sem[f"gate{j}_loaded"], 16)
                        r = end
            for m in range(AHEAD, 16):
                if m < AHEAD + 2:
                    eng.wait_ge(s.gate_summed, KR * (m - AHEAD + 1))
                else:
                    eng.wait_ge(s.mod_summed, m - 1)
                load_mod(m)
            for j in range(2):
                eng.wait_ge(s.mod_summed, 15 + j)
                load_rows(N_WOUT[j], a["lru_w_out"][0].rearrange("(k p) n -> p k n", p=P)
                          [:, 5 * j:5 * j + 5, :], 5, D)
            moe_loads(0, (s.gate_summed, 3 * KR), (s.state_ready, 1),
                      [(s.mixer_done, 1), (s.wout_half, 1), (s.logits_done, 1), (s.state_ready, 1)])
            extra_loads(0)
            for j in (2, 3, 0, 1, 4, 5):
                if j < 2:
                    eng.wait_ge(s.y_done, 1)
                elif j < 4:
                    eng.wait_ge(s.down_done, 2 * PAIRS)
                else:
                    eng.wait_ge(s.qkv_summed, 2 * (j - 3))
                load_rows(N_QKV + j, a["attn_w_qkv"][0].rearrange("(k p) n -> p k n", p=P)
                          [:, :, j * 512:(j + 1) * 512], KD, 512)
            for j in range(4):
                eng.wait_ge(s.qkv_summed, 2 * (j + 3))
                load_rows(N_WO + j, a["attn_w_o"][0].rearrange("(k p) n -> p k n", p=P)
                          [:, 2 * j:2 * j + 2, :], 2, D)
            moe_loads(1, (s.wo_done, 1), (s.w_ready, H),
                      [(s.wo_done, 3), (s.mixer_done, 2), (s.logits_done, 2), (s.wo_done, 2)])
            extra_loads(1)
            eng.wait_ge(s.x_new, 7)
            eng.dma_start(y_prompt[0], x[:, 0, :]).then_inc(s.outputs_stored, 16)
            eng.wait_ge(s.x_new, 8)
            eng.dma_start(y_sample[0], x[:, 1, :]).then_inc(s.outputs_stored, 16)
            eng.wait_ge(s.outputs_stored, 32)
            eng.wait_ge(s.kv_stored, 32)
            eng.wait_ge(s.state_stored, 16)

        @block.gpsimd
        def _(eng):
            for j in range(4):
                eng.wait_ge(*used(N_GATE + j - RING))
                eng.memset(ring[:, j, 0:2 * G_HALF], 0.0).then_inc(s.gate_zeroed, 1)
            for d in range(2):
                eng.wait_ge(s.gates_ready, KR * (d + 3))
                eng.wait_ge(s.xc_ready, KR)
                eng.tensor_tensor(IUs[d], IUs[d], xc, ALU.mult).then_inc(s.ix_ready, 1)
            def split(L):
                eng.wait_ge(s.xm_act, 4 * L + 3)
                eng.tensor_tensor(x32, x32, parts[0], ALU.subtract).then_inc(s.xm_pool, 1)
                eng.wait_ge(s.xm_act, 4 * L + 4)
                eng.wait_ge(s.xm_pool, 2 * L + 1)
                eng.tensor_tensor(parts[2], x32, parts[1], ALU.subtract).then_inc(s.xm_pool, 1)

            eng.wait_ge(s.state_copied, 1)
            eng.dma_start(new_state[0, 0].rearrange("d (c p) -> (d c) p", p=P), hlT[:, :])\
               .then_inc(s.state_stored, 16)
            split(0)
            eng.wait_ge(s.qkv_act, 6)
            eng.dma_start(new_k[0, 0].rearrange("t h e -> t (h e)"), qkv[:, 1, 0]).then_inc(s.kv_stored, 16)
            eng.dma_start(new_v[0, 0].rearrange("t h e -> t (h e)"), qkv[:, 2, 0]).then_inc(s.kv_stored, 16)
            split(1)

        @block.tensor
        def _(eng):
            def mm(out, lhsT, rhs, first, last):
                return eng.matmul(out, lhsT, rhs, start=first, stop=last, skip_group_check=True)

            def norm_in(n):
                for b in range(4):
                    st, half = divmod(b, 2)
                    eng.wait_ge(s.xn_ready, 2 * n + st + 1)
                    for i in range(4):
                        k = half * 4 + i
                        ins = eng.transpose(PS[:, 4 + b, i * P:(i + 1) * P],
                                            junk2[:, st, k * P:(k + 1) * P], ident)
                    ins.then_inc(s.xT_turned, 1)
                eng.wait_ge(s.hT_dve, 2 * (n + 1))
                eng.wait_ge(s.hT_act, 2 * (n + 1))

            def sum_ggb(n, banks=(4, 5, 6, 7)):
                for b in range(4):
                    eng.wait_ge(s.diag_ready, 4 * n + b + 1)
                    if banks[b] in banks[:b]:
                        eng.wait_ge(s.ggb_ready, 4 * n + b - 1)
                    for i in range(4):
                        ins = mm(PS[:, banks[b], i * P:(i + 1) * P], ones, diag[:, 4 * b + i, :], i == 0, True)
                    ins.then_inc(s.ggb_summed, 1)
                eng.wait_ge(s.ggb_ready, 4 * (n + 1))

            eng.wait_ge(s.consts_loaded, 16)
            eng.wait_ge(s.rows_loaded, 16 * ROW_LOADS)
            for i, (n, at) in enumerate(ROW_TILES):
                ins = eng.transpose(PS[:, 7, at:at + n], rows[0:n, i, :], ident[0:n, 0:n])
            ins.then_inc(s.vecs_turned, 1)

            def sum_mod(m):
                loaded(eng, N_MOD[m])
                if m == 2:
                    mod_copied(eng, 0)
                if m > EARLY:
                    mod_copied(eng, m - 1)
                w = ring_view(N_MOD[m], KD, MB)
                for half in range(2):
                    for k in range(KD):
                        g = 32 * (k % 4)
                        ins = mm(PS[g:g + 32, mod_bank(m) + half, 0:MB // 2], condT[:, k, :],
                                 w[:, k, half * MB // 2:(half + 1) * MB // 2], k < 4, k >= 4)
                ins.then_inc(s.mod_summed, 1)

            def turn_mod(m):
                mod_copied(eng, m)
                for i in range(6):
                    at = 2 * (m * 6 + i)
                    ins = mm(PS[:, 6, at:at + 2], mod_rows(m)[:, i // 3, i % 3 * P:(i % 3 + 1) * P],
                             con[:, C_SEL:C_SEL + 2], True, True)
                ins.then_inc(s.mod_done, 1)

            eng.wait_ge(s.cond_ready, 1)
            for m in range(EARLY):
                sum_mod(m)
            for m in range(EARLY):
                turn_mod(m)

            eng.wait_ge(s.mods_ready, 1)
            norm_in(0)
            for c in range(2 * KR):
                n = N_WIN[c // 5]
                loaded(eng, n)
                if 4 <= c < 14:
                    eng.wait_ge(s.gelu_ready, c - 3)
                elif c >= 14:
                    eng.wait_ge(s.xr_ready, c - 13)
                w = ring_view(n, KD, HALF)
                for k in range(KD):
                    ins = mm(PS[:, c % 4, 0:T], w[:, k, c % 5 * P:(c % 5 + 1) * P], hT[:, k, :],
                             k == 0, k == KD - 1)
                ins.then_inc(s.win_done, 1)
                if c % 5 == 4:
                    for m in (EARLY + 2 * (c // 5), EARLY + 1 + 2 * (c // 5)):
                        sum_mod(m)
                        if m > EARLY:
                            turn_mod(m - 1)
            turn_mod(AHEAD - 1)
            eng.wait_ge(s.xc_ready, KR)
            for j in range(4):
                eng.wait_ge(sem[f"gate{j}_loaded"], 16 * GATE_DMAS)
                store = ring[:, j, 0:2 * G_HALF].rearrange("p (h n) -> p h n", h=2)
                for c in range(KR):
                    i = j * KR + c
                    if i >= len(GATE_BANKS):
                        eng.wait_ge(s.gates_ready, i - len(GATE_BANKS) + 1)
                    half, cc = divmod(c, 5)
                    for k in G_INPUTS[cc]:
                        at = G_OFF[k] + cc * P - G_START[k]
                        ins = mm(PS[:, GATE_BANKS[i % 5], 0:T], store[:, half, at:at + P], xc[:, half * 5 + k, :],
                                 k == G_INPUTS[cc][0], k == G_INPUTS[cc][-1])
                    ins.then_inc(s.gate_summed, 1)
                    if i == 2 * KR + 4:
                        sum_mod(12)
                        turn_mod(11)
                if j:
                    sum_mod((0, 11, 13, 14)[j])
                if j > 1:
                    turn_mod(10 + j)
            sum_mod(15)
            turn_mod(14)
            turn_mod(15)
            eng.wait_ge(s.gates_ready, 4 * KR)
            for c in range(KR):
                loaded(eng, N_WOUT[c // 5])
                eng.wait_ge(s.yT_ready, c + 1)
                w = ring_view(N_WOUT[c // 5], 5, D)
                for st in range(NS):
                    for half in range(2):
                        ins = mm(PS[:, 2 * st + half, :], gel[:, c, st * P:(st + 1) * P],
                                 w[:, c % 5, half * 512:(half + 1) * 512], c == 0, c == KR - 1)
                if c == 4:
                    ins.then_inc(s.wout_half, 1)
                if c == 7:
                    sum_ggb(0, (4, 5, 4, 5))
                    eng.wait_ge(s.state_ready, 1)
                    eng.transpose(PS[0:2 * KR, 7, 0:P], hl[:, :, :].rearrange("p d c -> p (d c)"), ident)\
                       .then_inc(s.state_turned, 1)
                if c == KR - 1:
                    ins.then_inc(s.mixer_done, 1)

            def gather(sg_, j, Sb):
                eng.wait_ge(sg_.s_ready, j + 1)
                for half in range(2):
                    for i in range(4):
                        k = half * 4 + i
                        for part in range(3):
                            for st in range(NS):
                                ins = mm(PS[:, 6 + half, i * P:(i + 1) * P],
                                         parts[part][:, st * D + k * P:st * D + (k + 1) * P], Sb[:, st, :],
                                         part + st == 0, part + st == 3)
                    ins.then_inc(sg_.gathered, 1)

            def gate_up(sg_, j, places, wait_loaded):
                eng.wait_ge(sg_.xg_act, j + 1)
                eng.wait_ge(sg_.xg_dve, j + 1)
                wait_loaded(0)
                wait_loaded(1)
                for k in range(KD):
                    for e in range(2):
                        w = ring[:, places[e], k * 512:(k + 1) * 512]
                        ins = mm(PS[e * 64:(e + 1) * 64, 6, :], xg[:, k, e * 64:(e + 1) * 64], w,
                                 k == 0, k == KD - 1)
                ins.then_inc(sg_.gu_done, 1)

            def turn_hidden(sg_, j):
                eng.wait_ge(sg_.h_ready, j + 1)
                for fc in range(2):
                    ins = eng.transpose(PS[:, 7, fc * P:(fc + 1) * P], hE[:, fc * P:(fc + 1) * P], ident)
                ins.then_inc(sg_.h_turned, 1)

            def down(sg_, j, places, wait_loaded):
                eng.wait_ge(sg_.hT_ready, j + 1)
                wait_loaded(0)
                wait_loaded(1)
                for half in range(2):
                    for fc in range(2):
                        for e in range(2):
                            at = 4096 + fc * D + half * 512
                            ins = mm(PS[e * 64:(e + 1) * 64, 4 + half, :], hT2[:, fc, e * 64:(e + 1) * 64],
                                     ring[:, places[e], at:at + 512], fc == 0, fc == 1)
                    ins.then_inc(sg_.down_done, 1)

            def turn_weights(sg_, j, next_gathered):
                eng.wait_ge(sg_.sw_ready, j + 1)
                if next_gathered:
                    eng.wait_ge(sg_.xg_dve, j + 2)
                for st in range(NS):
                    ins = eng.transpose(PS[:, 7, 256 + st * P:256 + (st + 1) * P], Sw[:, st, :], ident)
                ins.then_inc(sg_.wT_turned, 1)

            def scatter(sg_, j, st):
                eng.wait_ge(sg_.o_act, j + 1)
                eng.wait_ge(sg_.o_dve, j + 1)
                eng.wait_ge(sg_.wT_ready, j + 1)
                for half in range(2):
                    ins = mm(PS[:, 2 * st + half, :], wT[:, st * P:(st + 1) * P],
                             osb[:, half * 512:(half + 1) * 512], False, False)
                ins.then_inc(sg_.scattered, 1)

            def moe(L):
                def static_gate_up(it, i):
                    places = (2 * i, 2 * i + 1)
                    gate_up(s, L * PAIRS + it * 2 + i, places, lambda e: eng.wait_ge(
                        sem[f"slot{places[e]}_loaded"], it * 32 + slot_value(N_EXPERT[L] + places[e])))

                n = 2 * L + 1
                norm_in(n)
                loaded(eng, N_ROUTER[L])
                w = ring_view(N_ROUTER[L], KD, E)
                for k in range(KD):
                    g = k % 2 * E
                    ins = mm(PS[g:g + E, 4, 0:T], w[:, k, :], hT[:, k, :], k < 2, k >= KD - 2)
                ins.then_inc(s.router_summed, 1)
                for b in range(4):
                    st, half = divmod(b, 2)
                    for i in range(4):
                        k = half * 4 + i
                        ins = eng.transpose(PS[:, XM_BANKS[b], i * P:(i + 1) * P],
                                            hT[:, k, st * P:(st + 1) * P], ident)
                    ins.then_inc(s.xm_turned, 1)
                eng.wait_ge(s.router_copied, L + 1)
                for st in range(NS):
                    ins = mm(PS[:, 7, st * E:(st + 1) * E], logitsT[:, st * P:(st + 1) * P],
                             con[:, C_FOLD:C_FOLD + E], True, True)
                ins.then_inc(s.logits_done, 1)
                eng.wait_ge(s.shared_loaded, 48 * (L + 1))
                w = shared_w[:, 0:4096].rearrange("p (k m f) -> p m k f", m=2, k=KD)
                for fc in range(2):
                    for m in range(2):
                        for k in range(KD):
                            ins = mm(PS[:, fc, m * T:(m + 1) * T], w[:, m, k, fc * P:(fc + 1) * P], hT[:, k, :],
                                     k == 0, k == KD - 1)
                    ins.then_inc(s.sh_summed, 1)
                    if fc == 0:
                        eng.wait_ge(s.router_copied, L + 1)
                        eng.wait_ge(s.xm_dve, 2 * L + 1)
                        eng.wait_ge(s.mask_ready, L + 1)
                        mm(PS[:, 4, 0:E], tri, mask[:, 0, :], True, True)
                        mm(PS[:, 4, E:2 * E], ones, mask[:, 0, :], True, False)
                        mm(PS[:, 4, E:2 * E], tri, mask[:, 1, :], False, True)
                        mm(PS[0:E, 5, 0:1], mask[:, 0, :], ones[:, 0:1], True, False)
                        mm(PS[0:E, 5, 0:1], mask[:, 1, :], ones[:, 0:1], False, True).then_inc(s.ranks_done, 1)
                eng.wait_ge(s.nb_ready, L + 1)
                mm(PS[0:E, 5, 8:9], tri[0:E, 0:E], nb[0:E, 0, 4:5], True, True)
                mm(PS[0:1, 5, 16:17], nb[0:E, 0, 4:5], ones[0:E, 0:1], True, True).then_inc(s.hi_done, 1)
                eng.wait_ge(s.xm_act, 4 * (L + 1))
                eng.wait_ge(s.xm_pool, 2 * (L + 1))
                gather(s, L * PAIRS, S[0])
                eng.wait_ge(s.pos_ready, L + 1)
                for st in range(NS):
                    eng.transpose(PS[0:E, 4, st * P:(st + 1) * P], pp[:, st, :], ident)
                    ins = eng.transpose(PS[0:E, 4, 256 + st * P:256 + (st + 1) * P], comb[:, st, :], ident)
                ins.then_inc(s.ppT_turned, 1)
                static_gate_up(0, 0)
                sum_ggb(n, (2, 3, 2, 3))
                eng.wait_ge(s.m_cols_ready, L + 1)
                eng.wait_ge(s.ppT_ready, L + 1)
                mm(PS[0:1, 5, 128:160], ecol[0:E, :], M[0:E, :], True, True)
                for st in range(NS):
                    mm(PS[:, 5, st * 32:(st + 1) * 32], ppT[0:E, st * P:(st + 1) * P], M[0:E, :], True, False)
                    mm(PS[:, 5, st * 32:(st + 1) * 32], ones[0:E, :], bM[0:E, :], False, True)
                    ins = mm(PS[:, 5, 64 + st * 32:64 + (st + 1) * 32], combT[0:E, st * P:(st + 1) * P],
                             M[0:E, :], True, True)
                ins.then_inc(s.xtable_done, 1)
                eng.wait_ge(s.sh_h, 2 * (L + 1))
                w = shared_w[:, 4096:6144].rearrange("p (c n) -> p c n", c=2)
                for st in range(NS):
                    for half in range(2):
                        for fc in range(2):
                            ins = mm(PS[:, 2 * st + half, :], shh[:, fc, st * P:(st + 1) * P],
                                     w[:, fc, half * 512:(half + 1) * 512], fc == 0, False)
                eng.wait_ge(s.xtable_ready, L + 1)

                def group(it, first, last):
                    for i in range(2):
                        j = L * PAIRS + it * 2 + i
                        places = (2 * i, 2 * i + 1)
                        more = not (last and i == 1)
                        if not (first and i == 0):
                            static_gate_up(it, i)
                        if not (first and i == 0):
                            scatter(s, j - 1, 0)
                        turn_hidden(s, j)
                        if not (first and i == 0):
                            scatter(s, j - 1, 1)
                        if more:
                            eng.wait_ge(s.hT_ready, j + 1)
                            gather(s, j + 1, S[(i + 1) % 2])
                        down(s, j, places, lambda e: eng.wait_ge(
                            sem[f"down{places[e]}_loaded"], it * 16 + (L * 256 + 16)))
                        turn_weights(s, j, more)

                group(0, True, False)
                with eng.Fori(1, PAIRS // 2 - 1) as it:
                    group(it, False, False)
                group(PAIRS // 2 - 1, False, True)
                for st in range(NS):
                    scatter(s, (L + 1) * PAIRS - 1, st)
                xs = extra[L]
                count = eng.value_load(xtab[0:1, 32:33], min_val=0, max_val=XITEMS)
                def extra_pair(i):
                    gather(xs, i, S[0])
                    gate_up(xs, i, (0, 1), lambda e: eng.wait_ge(xs.loaded, i * 96 + 96))
                    turn_hidden(xs, i)
                    down(xs, i, (0, 1), lambda e: None)
                    turn_weights(xs, i, False)
                    for st in range(NS):
                        scatter(xs, i, st)

                extra_pairs(eng, count, extra_pair)
                mm(PS[:, 7, 0:64], ident, ones[:, 0:64], True, True).then_inc(s.y_done, 1)

            moe(0)

            norm_in(2)
            for j in range(6):
                loaded(eng, N_QKV + j)
                w = ring_view(N_QKV + j, KD, 512)
                for st in range(NS):
                    if j >= 2:
                        eng.wait_ge((s.qkv_act, s.qkv_dve)[st], j - 1)
                    for k in range(KD):
                        ins = mm(PS[:, (2 * j + st) % 4, :], hT[:, k, st * P:(st + 1) * P], w[:, k, :],
                                 k == 0, k == KD - 1)
                    ins.then_inc(s.qkv_summed, 1)
            sum_ggb(2)
            eng.wait_ge(s.qkv_act, 6)
            eng.wait_ge(s.qkv_dve, 6)
            eng.wait_ge(s.cache_loaded, 32)
            def turn_qk(first, end):
                for g in range(first, end):
                    if g >= 4:
                        eng.wait_ge((s.qkT_act, s.qkT_dve)[g % 2], g // 2 - 1)
                    if g >= 6:
                        eng.wait_ge(s.roped, 2)
                    for i in range(4):
                        ins = eng.transpose(PS[:, 4 + g % 4, i * P:(i + 1) * P],
                                            TURNS[g][0][:, i * P:(i + 1) * P], ident)
                    ins.then_inc(s.qk_turned, 1)

            turn_qk(0, 10)
            eng.wait_ge(s.qkT_act, 5)
            eng.wait_ge(s.qkT_dve, 5)
            for step in range(H + 3):
                if step < H:
                    u = step
                    st = u // 4
                    if u >= 2:
                        eng.wait_ge(s.p_ready, u - 1)
                    for hh in range(2):
                        h = 2 * (u % 4) + hh
                        for comp in range(2):
                            lo = comp * HD
                            keys = kT[lo:lo + HD, h, 2, :] if st == 0 else \
                                kT[lo:lo + HD, h, 0:2, :].rearrange("p a t -> p (a t)")
                            ins = mm(PS[:, 2 * (u % 2) + comp, hh * T:hh * T + P * (st + 1)],
                                     qT[lo:lo + HD, h, st, :], keys, True, True)
                    ins.then_inc(s.sc_done, 1)
                if 2 <= step < H + 2:
                    u = step - 2
                    eng.wait_ge(s.w_ready, u + 1)
                    if u >= 2:
                        eng.wait_ge(s.wt_ready, u - 1)
                    for i in range(2 * (u // 4 + 1)):
                        ins = eng.transpose(PS[:, 4 + u % 2, i * P:(i + 1) * P],
                                            wmix[:, u % 2, i * P:(i + 1) * P], ident)
                    ins.then_inc(s.wt_turned, 1)
                if step >= 3:
                    u = step - 3
                    st = u // 4
                    eng.wait_ge(s.wt_ready, u + 1)
                    if u >= 2:
                        eng.wait_ge(s.o_copied, u - 1)
                    vals = [qkv[:, 2, 0]] if st == 0 else [kv_c[:, 1], qkv[:, 2, 1]]
                    for hh in range(2):
                        h = 2 * (u % 4) + hh
                        for kt, v in enumerate(vals):
                            at = (hh * len(vals) + kt) * P
                            ins = mm(PS[:, 6 + u % 2, hh * P:(hh + 1) * P], wmT[:, u % 2, at:at + P],
                                     v[:, h * P:(h + 1) * P], kt == 0, kt == len(vals) - 1)
                    ins.then_inc(s.pv_done, 1)
            for b in range(4):
                st, half = divmod(b, 2)
                eng.wait_ge(s.o_normed, 1)
                for i in range(4):
                    h = half * 4 + i
                    ins = eng.transpose(PS[:, 4 + b, i * P:(i + 1) * P], ot[:, st, h * P:(h + 1) * P], ident)
                ins.then_inc(s.oT_turned, 1)
            eng.wait_ge(s.oT_act, 2)
            eng.wait_ge(s.oT_dve, 2)
            for j in range(4):
                loaded(eng, N_WO + j)
                w = ring_view(N_WO + j, 2, D)
                for hh in range(2):
                    h = 2 * j + hh
                    for st in range(NS):
                        for half in range(2):
                            ins = mm(PS[:, 2 * st + half, :], oT[:, h, st * P:(st + 1) * P],
                                     w[:, hh, half * 512:(half + 1) * 512], h == 0, h == H - 1)
                ins.then_inc(s.wo_done if j < 3 else s.mixer_done, 1)
            moe(1)

        @block.scalar
        def _(eng):
            act = Steps(eng, s.act_step)

            eng.dma_start(con[:, :], a["constants"]).then_inc(s.consts_loaded, 16)
            for tile_, at, n, src in ROW_SOURCES:
                eng.dma_start(rows[at:at + n, tile_, :], src).then_inc(s.rows_loaded, 16)
            eng.dma_start(x[:, 0, :], a["x_prompt"][0]).then_inc(s.x_loaded, 16)
            eng.dma_start(x[:, 1, :], a["x_sample"][0]).then_inc(s.x_loaded, 16)
            eng.dma_start(bias[:, :, :], a["moe_router_bias"].partition_broadcast(P)).then_inc(s.vectors_loaded, 16)
            eng.dma_start(lamrow[:, :, :], a["attn_lambda"][0].partition_broadcast(P))\
               .then_inc(s.vectors_loaded, 16)

            def norm_in(n):
                if n == 0:
                    eng.wait_ge(s.x_loaded, 32)
                    eng.wait_ge(s.consts_loaded, 16)
                for st in range(NS):
                    act.settle()
                    if n:
                        eng.wait_ge(s.x_new, 2 * (n - 1) + st + 1)
                    act.keep(eng.activation(junk[:, :], x[:, st, :], ACT.Square, accum_out=stat[:, 0, st:st + 1]))
                    act.settle()
                    eng.activation(stat[:, 1, st:st + 1], stat[:, 0, st:st + 1], ACT.Sqrt, scale=1.0 / D, bias=epsc)\
                       .then_inc(s.rms_in, 1)
                if n == 0:
                    eng.wait_ge(s.mods_ready, 1)
                for b in (1, 3):
                    st, half = divmod(b, 2)
                    eng.wait_ge(s.xT_turned, 4 * n + b + 1)
                    for i in range(4):
                        k = half * 4 + i
                        ins = eng.activation(hT[:, k, st * P:(st + 1) * P], PS[:, 4 + b, i * P:(i + 1) * P],
                                             ACT.Identity, scale=amod[:, n, k, st:st + 1],
                                             bias=bmod(n)[:, k, st:st + 1])
                    ins.then_inc(s.hT_act, 1)

            def copy_ggb(n, banks=(4, 5, 6, 7)):
                for b in range(4):
                    eng.wait_ge(s.ggb_summed, 4 * n + b + 1)
                    eng.copy(ggb[:, b // 2, b % 2 * 512:(b % 2 + 1) * 512], PS[:, banks[b], :]).then_inc(s.ggb_ready, 1)

            def norm_out(n):
                eng.wait_ge(s.mixer_done if n % 2 == 0 else s.y_done, n // 2 + 1)
                for st in range(NS):
                    act.settle()
                    act.keep(eng.activation(junk[:, :], Y[:, st, :], ACT.Square, accum_out=stat[:, 2, st:st + 1]))
                    act.settle()
                    eng.activation(stat[:, 3, st:st + 1], stat[:, 2, st:st + 1], ACT.Sqrt, scale=1.0 / D, bias=epsc)\
                       .then_inc(s.rms_out, 1)

            def copy_mod(m, halves):
                eng.wait_ge(s.mod_summed, m + 1)
                mod_place_free(eng, m)
                b = mod_bank(m)
                eng.copy(mod_rows(m)[:, 0:halves], PS[:, b:b + halves, 0:MB // 2]).then_inc(s.mod_act, 1)

            eng.wait_ge(s.vecs_ready, 2)
            eng.activation(condT[:, :, 0:NS].rearrange("p k s -> p s k"),
                           vecs[:, 0, 64:80].rearrange("p (s k) -> p s k", s=NS), ACT.Silu)\
               .then_inc(s.cond_ready, 1)
            eng.wait_ge(s.dve_first, 2)
            eng.activation(sp[:, 1, :], sp[:, 0, :], ACT.Exp).then_inc(s.exps_done, 1)
            eng.activation(lam[:, 2:4], lam[:, 0:2], ACT.Exp).then_inc(s.exps_done, 1)
            for m in range(EARLY):
                copy_mod(m, 1)
            norm_in(0)
            for c in range(KR):
                eng.wait_ge(s.win_done, c + 1)
                eng.activation(gel[:, c, :], PS[:, c % 4, 0:T], ACT.Gelu_apprx_tanh).then_inc(s.gelu_ready, 1)
            for m in (7, 8, 9, 10):
                copy_mod(m, 2)
            for g in range(2):
                for d in range(2):
                    for c in range(KR):
                        i = (2 * g + d) * KR + c
                        eng.wait_ge(s.gate_summed, i + 1)
                        eng.activation((RAs, IUs)[g][d][:, c, :], PS[:, GATE_BANKS[i % 5], 0:T], ACT.Sigmoid,
                                       bias=gate_bias(2 * d + g, c)).then_inc(s.gates_ready, 1)
                if g == 0:
                    eng.wait_ge(s.decay_ready, 1)
                    eng.wait_ge(s.xc_ready, KR)
                    eng.wait_ge(s.win_done, 2 * KR)
                    act.settle()
                    eng.wait_ge(s.gates_ready, 2 * KR)
                    for i in range(2 * KR):
                        d, c = divmod(i, KR)
                        la = sp[:, 5, i:i + 1]
                        eng.activation(Qs[d][c], RAs[d][:, c, :], ACT.Tanh, scale=la).then_inc(s.tanh_exp_done, 1)
                        eng.activation(RAs[d][:, c, :], RAs[d][:, c, :], ACT.Exp, scale=la)\
                           .then_inc(s.tanh_exp_done, 1)
            for i in range(2 * KR):
                d, c = divmod(i, KR)
                eng.wait_ge(s.q_ready, i + 1)
                eng.activation(Qs[d][c], Qs[d][c], ACT.Sqrt, scale=-1.0).then_inc(s.m_ready, 1)
            copy_mod(15, 2)
            copy_ggb(0, (4, 5, 4, 5))
            eng.wait_ge(s.state_turned, 1)
            eng.copy(hlT[:, :], PS[0:2 * KR, 7, 0:P]).then_inc(s.state_copied, 1)
            norm_out(0)

            def silu(sg_, j):
                eng.wait_ge(sg_.gu_done, j + 1)
                eng.activation(sg, PS[:, 6, 0:F], ACT.Silu).then_inc(sg_.silu_ready, 1)

            def copy_hidden(sg_, j):
                eng.wait_ge(sg_.h_turned, j + 1)
                eng.copy(hT2.rearrange("p f n -> p (f n)"), PS[:, 7, 0:F]).then_inc(sg_.hT_ready, 1)

            def copy_gathered(sg_, j):
                eng.wait_ge(sg_.gathered, 2 * j + 1)
                eng.copy(xg[:, 0:4, :].rearrange("p k n -> p (k n)"), PS[:, 6, :]).then_inc(sg_.xg_act, 1)

            def copy_down(sg_, j):
                eng.wait_ge(sg_.down_done, 2 * j + 1)
                eng.copy(osb[:, 0:512], PS[:, 4, :]).then_inc(sg_.o_act, 1)

            def moe(L):
                n = 2 * L + 1
                norm_in(n)
                eng.wait_ge(s.router_summed, L + 1)
                if L:
                    eng.wait_ge(s.kv_stored, 32)
                eng.copy(logitsT, PS[:, 4, 0:T]).then_inc(s.router_copied, 1)
                for b in (1, 3):
                    eng.wait_ge(s.xm_turned, 4 * L + b + 1)
                    eng.copy(x32[:, b * 512:(b + 1) * 512], PS[:, XM_BANKS[b], :]).then_inc(s.xm_act, 1)
                eng.wait_ge(s.logits_done, L + 1)
                eng.activation(scores, PS[:, 7, 0:NS * E].rearrange("p (s e) -> p s e", s=NS), ACT.Sigmoid)\
                   .then_inc(s.scores_ready, 1)
                act.settle()
                eng.wait_ge(s.xm_act, 4 * L + 2)
                eng.wait_ge(s.xm_dve, 2 * (L + 1))
                eng.copy(parts[0], x32).then_inc(s.xm_act, 1)
                eng.wait_ge(s.xm_pool, 2 * L + 1)
                eng.copy(parts[1], x32).then_inc(s.xm_act, 1)
                for fc in range(2):
                    eng.wait_ge(s.sh_summed, 2 * L + fc + 1)
                    eng.activation(shg[:, fc, :], PS[:, fc, 0:T], ACT.Silu).then_inc(s.sh_silu, 1)
                copy_gathered(s, L * PAIRS)
                eng.wait_ge(s.ppT_turned, L + 1)
                act.keep(eng.copy(ppT[0:E, :], PS[0:E, 4, 0:T]))
                eng.copy(combT[0:E, :], PS[0:E, 4, T:2 * T]).then_inc(s.ppT_ready, 1)
                copy_ggb(n, (2, 3, 2, 3))

                def group(it, last):
                    for i in range(2):
                        j = L * PAIRS + it * 2 + i
                        silu(s, j)
                        copy_hidden(s, j)
                        if not (last and i == 1):
                            copy_gathered(s, j + 1)
                        copy_down(s, j)

                with eng.Fori(0, PAIRS // 2 - 1) as it:
                    group(it, False)
                group(PAIRS // 2 - 1, True)
                xs = extra[L]
                eng.wait_ge(s.xtable_ready, L + 1)
                count = eng.value_load(xtab[0:1, 32:33], min_val=0, max_val=XITEMS)
                def extra_pair(i):
                    copy_gathered(xs, i)
                    silu(xs, i)
                    copy_hidden(xs, i)
                    copy_down(xs, i)

                extra_pairs(eng, count, extra_pair)
                norm_out(n)

            moe(0)

            eng.wait_ge(s.x_new, 4)
            eng.dma_start(kv_c[:, 0], a["cache_k"][0, 0].rearrange("t h e -> t (h e)")).then_inc(s.cache_loaded, 16)
            eng.dma_start(kv_c[:, 1], a["cache_v"][0, 0].rearrange("t h e -> t (h e)")).then_inc(s.cache_loaded, 16)
            norm_in(2)
            for j in range(6):
                eng.wait_ge(s.qkv_summed, 2 * j + 1)
                eng.copy(qkv[:, j // 2, 0, j % 2 * 512:(j % 2 + 1) * 512], PS[:, 2 * j % 4, :]).then_inc(s.qkv_act, 1)
            copy_ggb(2)
            for g in range(0, 10, 2):
                eng.wait_ge(s.qk_turned, g + 1)
                eng.copy(TURNS[g][1], PS[:, 4 + g % 4, :].rearrange("p (h t) -> p h t", h=4)).then_inc(s.qkT_act, 1)
            for step in range(H + 3):
                if step < H:
                    u = step
                    eng.wait_ge(s.nm_ready, u + 1)
                    if u >= 2:
                        eng.wait_ge(s.w_ready, u - 1)
                    n = P * (u // 4 + 1)
                    for i in range(4):
                        hh, comp = divmod(i, 2)
                        ins = eng.activation(pr[:, u % 2, i, 0:n],
                                             PS[:, 2 * (u % 2) + comp, hh * T:hh * T + n], ACT.Exp,
                                             scale=SCALE, bias=sst[:, 0, 2 * u + hh, comp:comp + 1],
                                             accum_out=sst[:, 1, 2 * u + hh, comp:comp + 1])
                        if i < 3:
                            act.keep(ins)
                    ins.then_inc(s.p_ready, 1)
                if 2 <= step < H + 2:
                    u = step - 2
                    eng.wait_ge(s.wt_turned, u + 1)
                    if u >= 2:
                        eng.wait_ge(s.pv_done, u - 1)
                    n = 2 * P * (u // 4 + 1)
                    eng.copy(wmT[:, u % 2, 0:n], PS[:, 4 + u % 2, 0:n]).then_inc(s.wt_ready, 1)
                if step >= 3:
                    u = step - 3
                    eng.wait_ge(s.o_copied, u + 1)
                    for hh in range(2):
                        h = 2 * (u % 4) + hh
                        if u:
                            eng.wait_ge(s.o_squared, 2 * u + hh - 1)
                        eng.activation(junk[:, hh * P:(hh + 1) * P], ot[:, u // 4, h * P:(h + 1) * P], ACT.Square,
                                       accum_out=sst[:, 3, 2 * u + hh, 0:1]).then_inc(s.o_squared, 1)
            eng.wait_ge(s.o_squared, 16)
            eng.activation(sst[:, 3, :, 1], sst[:, 3, :, 0], ACT.Sqrt, scale=1.0 / P, bias=epsc)\
               .then_inc(s.o_rms, 1)
            for b in (1, 3):
                st, half = divmod(b, 2)
                eng.wait_ge(s.oT_turned, b + 1)
                eng.activation(oT[:, 4 * half:4 * half + 4, st * P:(st + 1) * P],
                               PS[:, 4 + b, :].rearrange("p (h t) -> p h t", h=4), ACT.Copy,
                               scale=lam[:, 6:7]).then_inc(s.oT_act, 1)
            norm_out(2)
            moe(1)

        @block.vector
        def _(eng):
            dve = Steps(eng, s.dve_step)

            def norm_in(n):
                for st in range(NS):
                    eng.wait_ge(s.rms_in, 2 * n + st + 1)
                    dve.keep(eng.reciprocal(stat[:, 1, st:st + 1], stat[:, 1, st:st + 1]))
                    dve.settle()
                    eng.tensor_scalar(junk2[:, st, :], x[:, st, :], stat[:, 1, st:st + 1], None, ALU.mult)\
                       .then_inc(s.xn_ready, 1)
                for b in (0, 2):
                    st, half = divmod(b, 2)
                    eng.wait_ge(s.xT_turned, 4 * n + b + 1)
                    for i in range(4):
                        k = half * 4 + i
                        ins = eng.tensor_scalar(hT[:, k, st * P:(st + 1) * P], PS[:, 4 + b, i * P:(i + 1) * P],
                                                amod[:, n, k, st:st + 1], bmod(n)[:, k, st:st + 1],
                                                ALU.mult, ALU.add)
                    ins.then_inc(s.hT_dve, 1)

            def diagonals(n):
                eng.wait_ge(s.xT_turned, 4 * n + 4)
                for b in range(4):
                    for i in range(4):
                        ins = eng.tensor_scalar(diag[:, 4 * b + i, :], ident,
                                                gg[:, n, (b % 2) * 4 + i, b // 2:b // 2 + 1], None, ALU.mult)
                    ins.then_inc(s.diag_ready, 1)

            def residual(n):
                for st in range(NS):
                    eng.wait_ge(s.rms_out, 2 * n + st + 1)
                    dve.keep(eng.reciprocal(stat[:, 3, st:st + 1], stat[:, 3, st:st + 1]))
                    dve.settle()
                    dve.keep(eng.scalar_tensor_tensor(out=junk2[:, st, :], in0=Y[:, st, :],
                                                      scalar=stat[:, 3, st:st + 1], in1=ggb[:, st, :],
                                                      op0=ALU.mult, op1=ALU.mult))
                    dve.settle()
                    eng.tensor_tensor(x[:, st, :], x[:, st, :], junk2[:, st, :], ALU.add).then_inc(s.x_new, 1)

            eng.wait_ge(s.vecs_turned, 1)
            for i, (n, at) in enumerate(ROW_TILES):
                ins = eng.tensor_copy(vecs[:, i, 0:n], PS[:, 7, at:at + n])
            ins.then_inc(s.vecs_ready, 1)
            eng.memset(condT[:, :, :], 0.0).then_inc(s.vecs_ready, 1)
            eng.wait_ge(s.vecs_ready, 1)
            dve.keep(eng.tensor_scalar(sp[:, 4, :], neglam, -1.0, None, ALU.mult))
            dve.settle()
            eng.tensor_tensor(sp[:, 0, :], sp[:, 4, :], neglam, ALU.min).then_inc(s.dve_first, 1)
            eng.wait_ge(s.vectors_loaded, 32)
            dve.keep(eng.tensor_tensor(junk2[:, 0, 0:128].rearrange("p (a d) -> p a d", a=2),
                                       lamrow[:, 0:4:2, :], lamrow[:, 1:4:2, :], ALU.mult))
            dve.settle()
            eng.tensor_reduce(lam[:, 0:2], junk2[:, 0, 0:128].rearrange("p (a d) -> p a d", a=2), AX, ALU.add)\
               .then_inc(s.dve_first, 1)
            eng.wait_ge(s.exps_done, 1)
            dve.keep(eng.tensor_scalar(sp[:, 2, :], sp[:, 1, :], 2.0, None, ALU.add))
            dve.settle()
            dve.keep(eng.reciprocal(sp[:, 2, :], sp[:, 2, :]))
            dve.settle()
            dve.keep(eng.tensor_tensor(sp[:, 1, :], sp[:, 1, :], sp[:, 2, :], ALU.mult))
            dve.settle()
            dve.keep(eng.tensor_tensor(sp[:, 2, :], sp[:, 1, :], sp[:, 1, :], ALU.mult))
            dve.settle()
            dve.keep(eng.tensor_scalar(sp[:, 3, :], sp[:, 2, :], 1.0 / 17, 1.0 / 15, ALU.mult, ALU.add))
            for k in (13, 11, 9, 7, 5, 3, 1):
                dve.settle()
                dve.keep(eng.tensor_tensor(sp[:, 3, :], sp[:, 3, :], sp[:, 2, :], ALU.mult))
                dve.settle()
                dve.keep(eng.tensor_scalar(sp[:, 3, :], sp[:, 3, :], 1.0 / k, None, ALU.add))
            dve.settle()
            dve.keep(eng.scalar_tensor_tensor(out=sp[:, 3, :], in0=sp[:, 3, :], scalar=2.0, in1=sp[:, 1, :],
                                              op0=ALU.mult, op1=ALU.mult))
            dve.keep(eng.tensor_scalar(sp[:, 4, :], sp[:, 4, :], 0.0, None, ALU.max))
            dve.settle()
            dve.keep(eng.tensor_tensor(sp[:, 3, :], sp[:, 3, :], sp[:, 4, :], ALU.add))
            dve.settle()
            eng.tensor_scalar(sp[:, 5, :], sp[:, 3, :], -8.0, None, ALU.mult).then_inc(s.decay_ready, 1)
            eng.wait_ge(s.exps_done, 2)
            dve.keep(eng.tensor_tensor(lam[:, 5:6], lam[:, 3:4], lam[:, 2:3], ALU.subtract))
            dve.settle()
            eng.tensor_scalar(lam[:, 4:5], lam[:, 5:6], -LAM0, None, ALU.add).then_inc(s.lam_ready, 1)
            eng.tensor_scalar(lam[:, 6:7], vecs[:, 3, 20:21], 1.0 - LAM0, None, ALU.mult).then_inc(s.lam_ready, 1)
            def copy_mod(m, halves):
                eng.wait_ge(s.mod_summed, m + 1)
                mod_place_free(eng, m)
                b = mod_bank(m)
                eng.tensor_copy(mod_rows(m)[:, 2 - halves:2], PS[:, b + 2 - halves:b + 2, 0:MB // 2])\
                   .then_inc(s.mod_dve, 1)

            def adaln_vectors(first, end):
                lo, hi = 6 * first, 6 * end
                eng.wait_ge(s.mod_done, end)
                dve.keep(eng.tensor_tensor(modT.rearrange("p i m s -> p (i m) s")[:, lo:hi],
                                           PS[:, 6, 2 * lo:2 * hi].rearrange("p (m s) -> p m s", s=NS),
                                           bc(vecs[:, 1, lo:hi], 2, NS), ALU.add))
                dve.settle()

            def input_gain(n):
                L, q = divmod(n, 2)
                dve.keep(eng.scalar_tensor_tensor(out=amod[:, n], in0=modT[:, L, 24 * q + 8:24 * q + 16],
                                                  scalar=1.0, in1=bc(gvec(L, 2 * q), 2, NS),
                                                  op0=ALU.add, op1=ALU.mult))

            for m in range(EARLY):
                copy_mod(m, 1)
            adaln_vectors(0, EARLY)
            input_gain(0)
            dve.settle()
            eng.tensor_copy(lam[:, 7:8], epsc).then_inc(s.mods_ready, 1)

            norm_in(0)
            dve.keep(eng.memset(xpad[:, :, :, 0:2], 0.0))
            dve.keep(eng.memset(xpad[:, :, :, 130:132], 0.0))
            dve.settle()
            for m in range(EARLY, 7):
                copy_mod(m, 2)
            for c in range(KR):
                eng.wait_ge(s.win_done, KR + c + 1)
                eng.tensor_copy(xpad[:, c, :, 2:130], PS[:, (KR + c) % 4, 0:T].rearrange("p (s t) -> p s t", s=NS))\
                   .then_inc(s.xr_ready, 1)
                eng.wait_ge(s.xr_ready, c + 1)
                y = xc[:, c, :].rearrange("p (s t) -> p s t", s=NS)
                dve.keep(eng.tensor_scalar(y, xpad[:, c, :, 0:P], conv_w(0, c), conv_b(c), ALU.mult, ALU.add))
                for t in range(1, 4):
                    dve.settle()
                    ins = eng.scalar_tensor_tensor(out=y, in0=xpad[:, c, :, t:t + P], scalar=conv_w(t, c),
                                                   in1=y, op0=ALU.mult, op1=ALU.add)
                    if t < 3:
                        dve.keep(ins)
                ins.then_inc(s.xc_ready, 1)
            copy_mod(11, 2)
            for d in range(2):
                if d:
                    copy_mod(12, 2)
                for c in range(KR):
                    eng.wait_ge(s.tanh_exp_done, 2 * (d * KR + c + 1))
                    dve.keep(eng.tensor_tensor(sq[:, c % 2, :], RAs[d][:, c, :], RAs[d][:, c, :], ALU.mult))
                    dve.settle()
                    eng.scalar_tensor_tensor(out=Qs[d][c], in0=sq[:, c % 2, :], scalar=1.0, in1=Qs[d][c],
                                             op0=ALU.add, op1=ALU.mult).then_inc(s.q_ready, 1)
            copy_mod(13, 2)
            copy_mod(14, 2)
            for d in range(2):
                eng.wait_ge(s.ix_ready, d + 1)
                for c in range(KR):
                    eng.wait_ge(s.m_ready, d * KR + c + 1)
                    eng.tensor_tensor(IUs[d][:, c, :], IUs[d][:, c, :], Qs[d][c], ALU.mult).then_inc(s.u_ready, 1)
                    eng.wait_ge(s.u_ready, d * KR + c + 1)
                    out = Qs[1][c] if d else HF[:, c, :]
                    for st in range(NS):
                        cut = slice(st * P, (st + 1) * P)
                        A_, U_, O_ = RAs[d][:, c, cut], IUs[d][:, c, cut], out[:, cut]
                        if d:
                            A_, U_, O_ = A_[:, ::-1], U_[:, ::-1], O_[:, ::-1]
                        start = vecs[:, 3, d * KR + c:d * KR + c + 1] if st else 0.0
                        dve.keep(eng.tensor_tensor_scan(O_, A_, U_, start, ALU.mult, ALU.add))
                    if d:
                        dve.settle()
                        dve.keep(eng.tensor_tensor(HF[:, c, :], HF[:, c, :], out, ALU.add))
                        dve.settle()
                        eng.tensor_tensor(gel[:, c, :], gel[:, c, :], HF[:, c, :], ALU.mult).then_inc(s.yT_ready, 1)
                dve.settle()
                if d == 0:
                    dve.keep(eng.tensor_copy(hl[:, 0, :], HF[:, :, P - 1]))
            dve.keep(eng.tensor_copy(hl[:, 1, 0:KD], hT[:, :, 0]))
            eng.tensor_copy(hl[:, 1, KD:KR], junk[:, 0:(KR - KD) * T].rearrange("p (c t) -> p c t", t=T)[:, :, 0])\
               .then_inc(s.state_ready, 1)
            adaln_vectors(EARLY, 16)
            for n in range(1, 4):
                input_gain(n)
            for n in range(4):
                L, q = divmod(n, 2)
                dve.keep(eng.tensor_tensor(gg[:, n], modT[:, L, 24 * q + 16:24 * q + 24],
                                           bc(gvec(L, 2 * q + 1), 2, NS), ALU.mult))
            dve.settle()
            diagonals(0)
            residual(0)

            def one_hots(sg_, item, j, buf):
                eng.tensor_tensor(S[buf].rearrange("p s (e n) -> p s e n", e=2),
                                  bc(bc(iota, 1, 2), 1, NS),
                                  bc(posI[:, bass.ds(item, 2), :].rearrange("p e s -> p s e"), 3, 64),
                                  ALU.is_equal).then_inc(sg_.s_ready, 1)

            def weighted(sg_, item, j, buf):
                eng.wait_ge(sg_.s_ready, j + 1)
                eng.tensor_tensor(Sw.rearrange("p s (e n) -> p s e n", e=2),
                                  S[buf].rearrange("p s (e n) -> p s e n", e=2),
                                  bc(comI[:, bass.ds(item, 2), :].rearrange("p e s -> p s e"), 3, 64),
                                  ALU.mult).then_inc(sg_.sw_ready, 1)

            def hidden(sg_, j):
                eng.wait_ge(sg_.silu_ready, j + 1)
                eng.tensor_tensor(hE, sg, PS[:, 6, F:2 * F], ALU.mult).then_inc(sg_.h_ready, 1)

            def copy_gathered(sg_, j):
                eng.wait_ge(sg_.gathered, 2 * j + 2)
                eng.tensor_copy(xg[:, 4:8, :].rearrange("p k n -> p (k n)"), PS[:, 7, :]).then_inc(sg_.xg_dve, 1)

            def copy_down(sg_, j):
                eng.wait_ge(sg_.down_done, 2 * j + 2)
                eng.tensor_copy(osb[:, 512:1024], PS[:, 5, :]).then_inc(sg_.o_dve, 1)

            def copy_weights(sg_, j):
                eng.wait_ge(sg_.wT_turned, j + 1)
                eng.tensor_copy(wT, PS[:, 7, 256:512]).then_inc(sg_.wT_ready, 1)

            def route(L):
                eng.wait_ge(s.scores_ready, L + 1)
                eng.wait_ge(s.vectors_loaded, 32)
                dve.keep(eng.tensor_tensor(sel, scores, bc(bias[:, L, :], 1, NS), ALU.add))
                dve.settle()
                for st in range(NS):
                    for g in range(NG):
                        dve.keep(eng.max(gtop[:, st, g, :], sel[:, st, g * 8:(g + 1) * 8]))
                dve.settle()
                dve.keep(eng.tensor_tensor(gsc, gtop[:, :, :, 0], gtop[:, :, :, 1], ALU.add))
                dve.settle()
                for st in range(NS):
                    dve.keep(eng.max(gm8[:, st, :], gsc[:, st, :]))
                dve.settle()
                for st in range(NS):
                    dve.keep(eng.max_index(idx[:, st, :], gm8[:, st, :], gsc[:, st, :]))
                dve.settle()
                dve.keep(eng.tensor_copy(idxf, idx[:, :, :]))
                dve.settle()
                for st in range(NS):
                    dve.keep(eng.tensor_tensor(eq[:, st], bc(idxf[:, st, 0:TOPG], 1, NG), bc(iota[:, 0:NG], 2, TOPG),
                                               ALU.is_equal))
                dve.settle()
                dve.keep(eng.tensor_reduce(gmask, eq, AX, ALU.max))
                dve.settle()
                grouped = [v.rearrange("p s (g e) -> p (s g) e", g=NG) for v in (masked, sel)]
                gm = gmask.rearrange("p s g -> p (s g)")
                dve.keep(eng.tensor_tensor(grouped[0], grouped[1], bc(gm, 2, 8), ALU.mult))
                dve.keep(eng.tensor_scalar(gsc, gmask, -1.0, BIG, ALU.add, ALU.mult))
                dve.settle()
                dve.keep(eng.tensor_tensor(grouped[0], grouped[0], bc(gsc.rearrange("p s g -> p (s g)"), 2, 8),
                                           ALU.add))
                dve.settle()
                for st in range(NS):
                    dve.keep(eng.max(gm8[:, st, :], masked[:, st, :]))
                dve.settle()
                for st in range(NS):
                    dve.keep(eng.match_replace(rep[:, st, :], gm8[:, st, :], masked[:, st, :], -1.1 * BIG))
                dve.settle()
                eng.tensor_tensor(mask, rep, masked, ALU.is_lt).then_inc(s.mask_ready, 1)
                eng.wait_ge(s.mask_ready, L + 1)
                dve.keep(eng.tensor_tensor(comb, scores, mask, ALU.mult))
                dve.settle()
                dve.keep(eng.tensor_reduce(wsum[:, :, 0], comb, AX, ALU.add))
                dve.settle()
                dve.keep(eng.reciprocal(wsum[:, :, 1], wsum[:, :, 0]))
                dve.settle()
                dve.keep(eng.scalar_tensor_tensor(out=comb, in0=comb, scalar=ROUTED, in1=bc(wsum[:, :, 1], 2, E),
                                                  op0=ALU.mult, op1=ALU.mult))

            def moe(L):
                n = 2 * L + 1
                norm_in(n)
                if L:
                    eng.wait_ge(s.kv_stored, 32)
                for b in (0, 2):
                    eng.wait_ge(s.xm_turned, 4 * L + b + 1)
                    eng.tensor_copy(x32[:, b * 512:(b + 1) * 512], PS[:, XM_BANKS[b], :]).then_inc(s.xm_dve, 1)
                route(L)
                def shared_hidden(fc):
                    eng.wait_ge(s.sh_silu, 2 * L + fc + 1)
                    eng.tensor_tensor(shh[:, fc, :], shg[:, fc, :], PS[:, fc, T:2 * T], ALU.mult)\
                       .then_inc(s.sh_h, 1)

                shared_hidden(0)
                eng.wait_ge(s.ranks_done, L + 1)
                dve.settle()
                dve.keep(eng.tensor_tensor(pp, PS[:, 4, 0:NS * E].rearrange("p (s e) -> p s e", s=NS), mask,
                                           ALU.mult))
                dve.settle()
                dve.keep(eng.tensor_copy(comI[:, 0:E, :].rearrange("p e s -> p s e"), comb))
                eng.tensor_scalar(posI[:, 0:E, :].rearrange("p e s -> p s e"), pp, -1.0, None, ALU.add)\
                   .then_inc(s.pos_ready, 1)
                eng.wait_ge(s.ranks_done, L + 1)
                for i in range(3):
                    dve.keep(eng.tensor_scalar(nb[0:E, 0, i:i + 1], PS[0:E, 5, 0:1], float(SLOTS * (i + 1)), None,
                                               ALU.is_gt))
                dve.settle()
                dve.keep(eng.tensor_tensor(nb[0:E, 0, 3:4], nb[0:E, 0, 0:1], nb[0:E, 0, 1:2], ALU.add))
                dve.settle()
                eng.tensor_tensor(nb[0:E, 0, 4:5], nb[0:E, 0, 3:4], nb[0:E, 0, 2:3], ALU.add).then_inc(s.nb_ready, 1)
                eng.wait_ge(s.pos_ready, L + 1)
                one_hots(s, 0, L * PAIRS, 0)
                diagonals(n)
                shared_hidden(1)
                eng.wait_ge(s.hi_done, L + 1)
                eng.wait_ge(s.nb_ready, L + 1)
                dve.keep(eng.tensor_copy(nb[0:E, 0, 6:7], PS[0:E, 5, 8:9]))
                dve.keep(eng.tensor_copy(xtab[0:1, 32:33], PS[0:1, 5, 16:17]))
                dve.settle()
                dve.keep(eng.tensor_tensor(nb[0:E, 0, 5:6], nb[0:E, 0, 6:7], nb[0:E, 0, 4:5], ALU.subtract))
                dve.settle()
                dve.keep(eng.tensor_scalar(M[0:E, :], iota[0:E, 0:32], nb[0:E, 0, 6:7], None, ALU.is_lt))
                dve.keep(eng.tensor_scalar(bM[0:E, :], iota[0:E, 0:32], nb[0:E, 0, 5:6], None, ALU.is_lt))
                dve.settle()
                dve.keep(eng.tensor_tensor(M[0:E, :], M[0:E, :], bM[0:E, :], ALU.subtract))
                dve.settle()
                dve.keep(eng.tensor_scalar(bM[0:E, :], iota[0:E, 0:32], nb[0:E, 0, 5:6], 1.0, ALU.subtract, ALU.add))
                dve.settle()
                eng.scalar_tensor_tensor(out=bM[0:E, :], in0=bM[0:E, :], scalar=-float(SLOTS), in1=M[0:E, :],
                                         op0=ALU.mult, op1=ALU.mult).then_inc(s.m_cols_ready, 1)
                copy_gathered(s, L * PAIRS)
                eng.wait_ge(s.xtable_done, L + 1)
                dve.keep(eng.tensor_copy(xtab[0:1, 0:32], PS[0:1, 5, 128:160]))
                dve.keep(eng.tensor_scalar(posI[:, E:ITEMS, :].rearrange("p e s -> p s e"),
                                           PS[:, 5, 0:64].rearrange("p (s x) -> p s x", s=NS), -1.0, None, ALU.add))
                eng.tensor_copy(comI[:, E:ITEMS, :].rearrange("p e s -> p s e"),
                                PS[:, 5, 64:128].rearrange("p (s x) -> p s x", s=NS)).then_inc(s.xtable_ready, 1)
                eng.wait_ge(s.xtable_ready, L + 1)
                eng.wait_ge(s.pos_ready, L + 1)
                dve.settle()

                def group(it, last):
                    for i in range(2):
                        j = L * PAIRS + it * 2 + i
                        item = it * 4 + 2 * i
                        if not (last and i == 1):
                            one_hots(s, item + 2, j + 1, (i + 1) % 2)
                        weighted(s, item, j, i)
                        hidden(s, j)
                        if not (last and i == 1):
                            copy_gathered(s, j + 1)
                        copy_down(s, j)
                        copy_weights(s, j)

                with eng.Fori(0, PAIRS // 2 - 1) as it:
                    group(it, False)
                group(PAIRS // 2 - 1, True)
                xs = extra[L]
                eng.wait_ge(s.scattered, 2 * (L + 1) * PAIRS)
                count = eng.value_load(xtab[0:1, 32:33], min_val=0, max_val=XITEMS)
                def extra_pair(i):
                    one_hots(xs, i * 2 + E, i, 0)
                    weighted(xs, i * 2 + E, i, 0)
                    copy_gathered(xs, i)
                    hidden(xs, i)
                    copy_down(xs, i)
                    copy_weights(xs, i)

                extra_pairs(eng, count, extra_pair)
                residual(n)

            moe(0)

            def rope_in_place(w):
                src = qkv[:, w, 1].rearrange("p (h a b j) -> p h a b j", h=2 * H, a=2, b=2)
                rot = rope[:, w].rearrange("p (h a b j) -> p h a b j", h=2 * H, a=2, b=2)
                sn = con[:, C_SIN:C_SIN + HD].rearrange("p (a b j) -> p a b j", a=2, b=2)
                for b in range(2):
                    dve.keep(eng.tensor_tensor(rot[:, :, :, b, :], src[:, :, :, 1 - b, :],
                                               bc(sn[:, :, b, :], 1, 2 * H), ALU.mult))
                dve.settle()
                src = qkv[:, w, 1].rearrange("p (h d) -> p h d", h=2 * H)
                dve.keep(eng.tensor_tensor(src, src, bc(con[:, C_COS:C_COS + HD], 1, 2 * H), ALU.mult))
                dve.settle()
                eng.tensor_tensor(qkv[:, w, 1], qkv[:, w, 1], rope[:, w], ALU.add).then_inc(s.roped, 1)

            norm_in(2)
            diagonals(2)
            for j in range(6):
                eng.wait_ge(s.qkv_summed, 2 * j + 2)
                eng.tensor_copy(qkv[:, j // 2, 1, j % 2 * 512:(j % 2 + 1) * 512], PS[:, (2 * j + 1) % 4, :])\
                   .then_inc(s.qkv_dve, 1)
                if j in (1, 3):
                    eng.wait_ge(s.qkv_dve, j + 1)
                    rope_in_place(j // 2)
            for g in (1, 3, 5):
                eng.wait_ge(s.qk_turned, g + 1)
                eng.tensor_copy(TURNS[g][1], PS[:, 4 + g % 4, :].rearrange("p (h t) -> p h t", h=4))\
                   .then_inc(s.qkT_dve, 1)
            for g in (7, 9):
                eng.wait_ge(s.qk_turned, g + 1)
                eng.tensor_copy(TURNS[g][1], PS[:, 4 + g % 4, :].rearrange("p (h t) -> p h t", h=4))\
                   .then_inc(s.qkT_dve, 1)
            eng.wait_ge(s.lam_ready, 2)
            for step in range(H + 3):
                if step < H:
                    u = step
                    eng.wait_ge(s.sc_done, u + 1)
                    n = P * (u // 4 + 1)
                    b0 = 2 * (u % 2)
                    top = sst[:, 0, 2 * u:2 * u + 2, :]
                    dve.keep(eng.tensor_reduce(
                        top, PS[:, b0:b0 + 2, :].rearrange("p c (h n) -> p h c n", h=2)[:, :, :, 0:n], AX, ALU.max))
                    dve.settle()
                    eng.tensor_scalar(top, top, -SCALE, None, ALU.mult).then_inc(s.nm_ready, 1)
                if 1 <= step <= H:
                    u = step - 1
                    n = P * (u // 4 + 1)
                    eng.wait_ge(s.p_ready, u + 1)
                    dve.keep(eng.reciprocal(sst[:, 2, 2 * u:2 * u + 2, :], sst[:, 1, 2 * u:2 * u + 2, :]))
                    dve.settle()
                    for hh in range(2):
                        p1 = pr[:, u % 2, 2 * hh + 1, 0:n]
                        dve.keep(eng.tensor_scalar(p1, p1, sst[:, 2, 2 * u + hh, 1:2], lam[:, 4:5],
                                                   ALU.mult, ALU.mult))
                    dve.settle()
                    if u >= 2:
                        eng.wait_ge(s.wt_turned, u - 1)
                    for hh in range(2):
                        ins = eng.scalar_tensor_tensor(out=wmix[:, u % 2, hh * n:(hh + 1) * n],
                                                       in0=pr[:, u % 2, 2 * hh, 0:n],
                                                       scalar=sst[:, 2, 2 * u + hh, 0:1],
                                                       in1=pr[:, u % 2, 2 * hh + 1, 0:n],
                                                       op0=ALU.mult, op1=ALU.add)
                        if hh == 0:
                            dve.keep(ins)
                    ins.then_inc(s.w_ready, 1)
                if step >= 3:
                    u = step - 3
                    eng.wait_ge(s.pv_done, u + 1)
                    eng.tensor_copy(ot[:, u // 4, u % 4 * T:(u % 4 + 1) * T], PS[:, 6 + u % 2, 0:T])\
                       .then_inc(s.o_copied, 1)
            eng.wait_ge(s.o_rms, 1)
            dve.keep(eng.reciprocal(sst[:, 3, :, 1], sst[:, 3, :, 1]))
            eng.wait_ge(s.o_copied, H)
            dve.settle()
            v = ot.rearrange("p s (h e) -> p (s h) e", h=H)
            eng.tensor_tensor(v, v, bc(sst[:, 3, :, 1], 2, P), ALU.mult).then_inc(s.o_normed, 1)
            for b in (0, 2):
                st, half = divmod(b, 2)
                eng.wait_ge(s.oT_turned, b + 1)
                eng.tensor_scalar(oT[:, 4 * half:4 * half + 4, st * P:(st + 1) * P],
                                  PS[:, 4 + b, :].rearrange("p (h t) -> p h t", h=4), lam[:, 6:7], None,
                                  ALU.mult).then_inc(s.oT_dve, 1)
            residual(2)
            moe(1)


_INS = ["x_prompt", "x_sample", "c", "state_lru", "cache_k", "cache_v", "c_ctx", "mod_w", "mod_b", "norm_g",
        "lru_w_in", "lru_conv_w", "lru_conv_b", "lru_gate_w", "lru_gate_b", "lru_lambda", "lru_w_out",
        "attn_w_qkv", "attn_lambda", "attn_subln", "attn_w_o", "moe_router", "moe_router_bias", "moe_w_gate",
        "moe_w_up", "moe_w_down", "shared_w_gate", "shared_w_up", "shared_w_down"]
_OUTS = [(1, P, D), (1, P, D), (1, 1, 2, R), (1, 1, P, H, 2 * HD), (1, 1, P, H, 2 * HD)]


def kernel(**inputs):
    import concourse.bacc as bacc
    from concourse.bass_utils import run_bass_kernel_spmd

    nc = bacc.Bacc("TRN2", target_bir_lowering=False, num_devices=1)
    arrays = {name: np.ascontiguousarray(inputs[name]) for name in _INS}
    arrays["constants"] = constants()
    a = {name: nc.dram_tensor(f"in_{name}", v.shape, F32, kind="ExternalInput").ap() for name, v in arrays.items()}
    outs = [nc.dram_tensor(f"out_{i}", shape, F32, kind="ExternalOutput").ap() for i, shape in enumerate(_OUTS)]
    trunk(nc, a, outs)
    r = run_bass_kernel_spmd(nc, [{f"in_{name}": v for name, v in arrays.items()}], core_ids=[0])
    return tuple(r.results[0][f"out_{i}"] for i in range(len(_OUTS)))
```
